# Optimizing a Trainium2 kernel written in Bass

```python
import math
import jax, jax.numpy as jnp
from jax import lax
import numpy as np

D_MODEL = 1024
BATCH = 1
SEQ = 512
DEPTH = 4

N_MIXERS = 4
EPS = 1e-6
CONV_WIDTH = 1024
CONV_K = 3
FOX_HEADS = 8
FOX_HEAD_DIM = 128
FOX_WIDTH = FOX_HEADS * FOX_HEAD_DIM
Q_BLOCK = 128
GDN_HEADS = 8
GDN_HEAD_DIM = 128
GDN_WIDTH = GDN_HEADS * GDN_HEAD_DIM
GDN_CONV_K = 4
GDN_CHUNK = 64
SWA_HEADS = 16
SWA_KV_HEADS = 4
SWA_GROUP = SWA_HEADS // SWA_KV_HEADS
SWA_HEAD_DIM = 64
SWA_WIDTH = SWA_HEADS * SWA_HEAD_DIM
SWA_KV_WIDTH = SWA_KV_HEADS * SWA_HEAD_DIM
WINDOW = 128
ROPE_THETA = 10000.0

N_CONV_LAYERS = (DEPTH + 3) // 4
N_FOX_LAYERS = (DEPTH + 2) // 4
N_GDN_LAYERS = (DEPTH + 1) // 4
N_SWA_LAYERS = DEPTH // 4


def rms_norm(x, w):
    x32 = x.astype(jnp.float32)
    y = x32 * lax.rsqrt(jnp.mean(x32 * x32, axis=-1, keepdims=True) + EPS)
    return (y * w.astype(jnp.float32)).astype(x.dtype)

def causal_conv(u, w):
    K = w.shape[0]
    S = u.shape[1]
    up = jnp.pad(u, ((0, 0), (K - 1, 0), (0, 0)))
    out = up[:, 0:S] * w[0]
    for k in range(1, K):
        out = out + up[:, k:k + S] * w[k]
    return out

def rope(x, positions):
    d = x.shape[-1]
    half = d // 2
    inv_freq = ROPE_THETA ** (-jnp.arange(half, dtype=jnp.float32) / half)
    ang = positions.astype(jnp.float32)[..., None] * inv_freq
    cos = jnp.cos(ang)[:, :, None, :]
    sin = jnp.sin(ang)[:, :, None, :]
    x32 = x.astype(jnp.float32)
    x1, x2 = x32[..., :half], x32[..., half:]
    return jnp.concatenate([x1 * cos - x2 * sin, x2 * cos + x1 * sin], axis=-1).astype(x.dtype)

def conv_mixer(h, w_in, w_conv, w_out):
    proj = h @ w_in
    b_gate, c_gate, v, z = jnp.split(proj, 4, axis=-1)
    y = b_gate * causal_conv(c_gate * v, w_conv)
    return (y * jax.nn.silu(z)) @ w_out

def fox_mixer(h, w_in, b_f, w_out):
    B_, S, _ = h.shape
    H, d = FOX_HEADS, FOX_HEAD_DIM
    proj = h @ w_in
    q, k, v, z, f_logit = jnp.split(proj, [FOX_WIDTH, 2 * FOX_WIDTH, 3 * FOX_WIDTH, 4 * FOX_WIDTH], axis=-1)
    q = q.reshape(B_, S, H, d)
    k = k.reshape(B_, S, H, d)
    v = v.reshape(B_, S, H, d)
    log_f = jax.nn.log_sigmoid((f_logit + b_f).astype(jnp.float32))
    c = jnp.cumsum(log_f, axis=1)
    c_keys = c.transpose(0, 2, 1)
    nblk = S // Q_BLOCK
    q_blocks = q.reshape(B_, nblk, Q_BLOCK, H, d).transpose(1, 0, 2, 3, 4)
    c_blocks = c.reshape(B_, nblk, Q_BLOCK, H).transpose(1, 0, 3, 2)
    scale = 1.0 / math.sqrt(d)
    k_pos = jnp.arange(S)

    def block(args):
        i, q_i, c_i = args
        s = jnp.einsum('bqhd,bkhd->bhqk', q_i, k).astype(jnp.float32) * scale
        decay = c_i[..., :, None] - c_keys[:, :, None, :]
        q_pos = i * Q_BLOCK + jnp.arange(Q_BLOCK)
        mask = k_pos[None, :] <= q_pos[:, None]
        logits = jnp.where(mask, s + decay, -jnp.inf)
        p = jax.nn.softmax(logits, axis=-1)
        return jnp.einsum('bhqk,bkhd->bqhd', p.astype(v.dtype), v)

    o = lax.map(block, (jnp.arange(nblk), q_blocks, c_blocks))
    o = o.transpose(1, 0, 2, 3, 4).reshape(B_, S, FOX_WIDTH)
    return (o * jax.nn.silu(z)) @ w_out

def chunk_gated_delta(q, k, v, g, beta):
    B_, S, H, dk = q.shape
    dv = v.shape[-1]
    C = GDN_CHUNK
    n = S // C
    f32 = jnp.float32

    def chunks(t):
        return t.astype(f32).reshape(B_, n, C, H, -1).transpose(0, 3, 1, 2, 4)

    q, k, v = chunks(q), chunks(k), chunks(v)
    beta = beta.astype(f32).reshape(B_, n, C, H).transpose(0, 3, 1, 2)
    g_cum = jnp.cumsum(g.astype(f32).reshape(B_, n, C, H).transpose(0, 3, 1, 2), axis=-1)
    k_beta = k * beta[..., None]
    v_beta = v * beta[..., None]
    idx = jnp.arange(C)
    causal = idx[:, None] >= idx[None, :]
    strict = idx[:, None] > idx[None, :]
    diff = g_cum[..., :, None] - g_cum[..., None, :]
    decay = jnp.where(causal, jnp.exp(jnp.where(causal, diff, 0.0)), 0.0)
    L = jnp.where(strict, jnp.einsum('bhnid,bhnjd->bhnij', k_beta, k) * decay, 0.0)
    eye = jnp.eye(C, dtype=f32)
    T = lax.linalg.triangular_solve(eye + L, jnp.broadcast_to(eye, L.shape), left_side=True, lower=True, unit_diagonal=True)
    u = T @ v_beta
    w = T @ (k_beta * jnp.exp(g_cum)[..., None])
    qk = jnp.where(causal, jnp.einsum('bhnid,bhnjd->bhnij', q, k) * decay, 0.0)
    g_last = g_cum[..., -1]
    k_dec = k * jnp.exp(g_last[..., None] - g_cum)[..., None]
    q_dec = q * jnp.exp(g_cum)[..., None]

    def to_scan(t):
        return jnp.moveaxis(t, 2, 0)

    def step(state, xs):
        qd, kd, u_c, w_c, qk_c, gl = xs
        v_new = u_c - w_c @ state
        o = qd @ state + qk_c @ v_new
        state = state * jnp.exp(gl)[..., None, None] + jnp.einsum('bhck,bhcv->bhkv', kd, v_new)
        return state, o

    state0 = jnp.zeros((B_, H, dk, dv), f32)
    xs = (to_scan(q_dec), to_scan(k_dec), to_scan(u), to_scan(w), to_scan(qk), to_scan(g_last))
    _, o = lax.scan(step, state0, xs)
    return o.transpose(1, 0, 3, 2, 4).reshape(B_, S, H, dv)

def gdn_mixer(h, w_in, w_conv, a_log, dt_bias, w_onorm, w_out):
    B_, S, _ = h.shape
    H, d = GDN_HEADS, GDN_HEAD_DIM
    proj = h @ w_in
    qkv, z, beta_logit, a_logit = jnp.split(proj, [3 * GDN_WIDTH, 4 * GDN_WIDTH, 4 * GDN_WIDTH + H], axis=-1)
    qkv = jax.nn.silu(causal_conv(qkv, w_conv))
    q, k, v = jnp.split(qkv, 3, axis=-1)
    q = q.reshape(B_, S, H, d).astype(jnp.float32)
    k = k.reshape(B_, S, H, d).astype(jnp.float32)
    v = v.reshape(B_, S, H, d)
    q = q * lax.rsqrt(jnp.sum(q * q, axis=-1, keepdims=True) + EPS) * (1.0 / math.sqrt(d))
    k = k * lax.rsqrt(jnp.sum(k * k, axis=-1, keepdims=True) + EPS)
    beta = jax.nn.sigmoid(beta_logit.astype(jnp.float32))
    g = -jnp.exp(a_log.astype(jnp.float32)) * jax.nn.softplus(a_logit.astype(jnp.float32) + dt_bias.astype(jnp.float32))
    o = chunk_gated_delta(q, k, v, g, beta)
    o = o * lax.rsqrt(jnp.mean(o * o, axis=-1, keepdims=True) + EPS) * w_onorm.astype(jnp.float32)
    o = o.reshape(B_, S, GDN_WIDTH).astype(h.dtype)
    return (o * jax.nn.silu(z)) @ w_out

def swa_mixer(h, positions, w_in, sinks, w_out):
    B_, S, _ = h.shape
    Hk, G, d = SWA_KV_HEADS, SWA_GROUP, SWA_HEAD_DIM
    proj = h @ w_in
    q, k, v, z = jnp.split(proj, [SWA_WIDTH, SWA_WIDTH + SWA_KV_WIDTH, SWA_WIDTH + 2 * SWA_KV_WIDTH], axis=-1)
    q = rope(q.reshape(B_, S, SWA_HEADS, d), positions)
    k = rope(k.reshape(B_, S, Hk, d), positions)
    v = v.reshape(B_, S, Hk, d)
    W = WINDOW
    nblk = S // W
    qb = q.reshape(B_, nblk, W, Hk, G, d)

    def band(t):
        tb = t.reshape(B_, nblk, W, Hk, d)
        prev = jnp.pad(tb, ((0, 0), (1, 0), (0, 0), (0, 0), (0, 0)))[:, :-1]
        return jnp.concatenate([prev, tb], axis=2)

    kk, vv = band(k), band(v)
    s = jnp.einsum('bnqhgd,bnkhd->bnhgqk', qb, kk).astype(jnp.float32) * (1.0 / math.sqrt(d))
    q_idx = jnp.arange(W)[:, None] + W
    k_idx = jnp.arange(2 * W)[None, :]
    rel = q_idx - k_idx
    blk = jnp.arange(nblk)[:, None, None]
    mask = (rel >= 0) & (rel < WINDOW) & (blk * W + k_idx - W >= 0)
    logits = jnp.where(mask[None, :, None, None, :, :], s, -jnp.inf)
    sink = sinks.astype(jnp.float32).reshape(1, 1, Hk, G, 1, 1)
    m = jnp.maximum(jnp.max(logits, axis=-1, keepdims=True), sink)
    e = jnp.exp(logits - m)
    p = e / (jnp.sum(e, axis=-1, keepdims=True) + jnp.exp(sink - m))
    o = jnp.einsum('bnhgqk,bnkhd->bnqhgd', p.astype(vv.dtype), vv).reshape(B_, S, SWA_WIDTH)
    return (o * jax.nn.silu(z)) @ w_out

def first_inputs(seed: int = 0) -> dict:
    key = jax.random.key(seed)
    ks = jax.random.split(key, 24)
    f32 = jnp.float32
    D = D_MODEL

    def lin(k, shape):
        return jax.random.normal(k, shape, f32) * (shape[-2] ** -0.5)

    x = jax.random.normal(ks[0], (BATCH, SEQ, D), f32)
    offset = jax.random.randint(ks[1], (BATCH, 1), 0, 1024, dtype=jnp.int32)
    positions = offset + jnp.arange(SEQ, dtype=jnp.int32)[None, :]
    norm_w = 1.0 + 0.1 * jax.random.normal(ks[2], (DEPTH, D), f32)
    final_norm_w = 1.0 + 0.1 * jax.random.normal(ks[3], (D,), f32)
    conv_w_in = lin(ks[4], (N_CONV_LAYERS, D, 4 * CONV_WIDTH))
    conv_w_conv = jax.random.normal(ks[5], (N_CONV_LAYERS, CONV_K, CONV_WIDTH), f32) * (CONV_K ** -0.5)
    conv_w_out = lin(ks[6], (N_CONV_LAYERS, CONV_WIDTH, D))
    fox_w_in = lin(ks[7], (N_FOX_LAYERS, D, 4 * FOX_WIDTH + FOX_HEADS))
    fox_b_f = jax.random.uniform(ks[8], (N_FOX_LAYERS, FOX_HEADS), f32, 1.0, 5.0)
    fox_w_out = lin(ks[9], (N_FOX_LAYERS, FOX_WIDTH, D))
    gdn_w_in = lin(ks[10], (N_GDN_LAYERS, D, 4 * GDN_WIDTH + 2 * GDN_HEADS))
    gdn_w_conv = jax.random.normal(ks[11], (N_GDN_LAYERS, GDN_CONV_K, 3 * GDN_WIDTH), f32) * (GDN_CONV_K ** -0.5)
    gdn_a_log = jnp.log(jax.random.uniform(ks[12], (N_GDN_LAYERS, GDN_HEADS), f32, 1.0, 16.0))
    dt = jnp.exp(jax.random.uniform(ks[13], (N_GDN_LAYERS, GDN_HEADS), f32, math.log(1e-3), math.log(1e-1)))
    gdn_dt_bias = dt + jnp.log(-jnp.expm1(-dt))
    gdn_norm_w = 1.0 + 0.1 * jax.random.normal(ks[14], (N_GDN_LAYERS, GDN_HEAD_DIM), f32)
    gdn_w_out = lin(ks[15], (N_GDN_LAYERS, GDN_WIDTH, D))
    swa_w_in = lin(ks[16], (N_SWA_LAYERS, D, 2 * SWA_WIDTH + 2 * SWA_KV_WIDTH))
    swa_sinks = 0.5 * jax.random.normal(ks[17], (N_SWA_LAYERS, SWA_HEADS), f32)
    swa_w_out = lin(ks[18], (N_SWA_LAYERS, SWA_WIDTH, D))
    return {"x": x, "positions": positions, "norm_w": norm_w, "final_norm_w": final_norm_w,
            "conv_w_in": conv_w_in, "conv_w_conv": conv_w_conv, "conv_w_out": conv_w_out,
            "fox_w_in": fox_w_in, "fox_b_f": fox_b_f, "fox_w_out": fox_w_out,
            "gdn_w_in": gdn_w_in, "gdn_w_conv": gdn_w_conv, "gdn_a_log": gdn_a_log, "gdn_dt_bias": gdn_dt_bias,
            "gdn_norm_w": gdn_norm_w, "gdn_w_out": gdn_w_out,
            "swa_w_in": swa_w_in, "swa_sinks": swa_sinks, "swa_w_out": swa_w_out}

def first_block(x, positions, norm_w, final_norm_w, conv_w_in, conv_w_conv, conv_w_out,
              fox_w_in, fox_b_f, fox_w_out, gdn_w_in, gdn_w_conv, gdn_a_log, gdn_dt_bias,
              gdn_norm_w, gdn_w_out, swa_w_in, swa_sinks, swa_w_out):
    for i in range(DEPTH):
        h = rms_norm(x, norm_w[i])
        kind, j = i % N_MIXERS, i // N_MIXERS
        if kind == 0:
            y = conv_mixer(h, conv_w_in[j], conv_w_conv[j], conv_w_out[j])
        elif kind == 1:
            y = fox_mixer(h, fox_w_in[j], fox_b_f[j], fox_w_out[j])
        elif kind == 2:
            y = gdn_mixer(h, gdn_w_in[j], gdn_w_conv[j], gdn_a_log[j], gdn_dt_bias[j], gdn_norm_w[j], gdn_w_out[j])
        else:
            y = swa_mixer(h, positions, swa_w_in[j], swa_sinks[j], swa_w_out[j])
        x = x + y.astype(x.dtype)
    return rms_norm(x, final_norm_w)


DEPTH_2 = 1

N_MEM = 256
SB_HEADS = 8
SB_HEAD_DIM = 64
SB_WIDTH = SB_HEADS * SB_HEAD_DIM
ML_HEADS = 4
ML_HEAD_DIM = 128
ML_WIDTH = ML_HEADS * ML_HEAD_DIM
ML_CONV = 4
ML_CHUNK = 128
XA_HEADS = 4
XA_HEAD_DIM = 128
XA_WIDTH = XA_HEADS * XA_HEAD_DIM
N_BRANCH = 3
D_FF = 2816
FF_CONV = 3

IN_SIZES = (SB_WIDTH, SB_WIDTH, SB_WIDTH, ML_WIDTH, ML_WIDTH, ML_WIDTH, ML_WIDTH,
            ML_HEADS, ML_HEADS, XA_WIDTH, N_BRANCH * D_MODEL)
IN_TOTAL = sum(IN_SIZES)


def _rmsnorm(x, g):
    xf = x.astype(jnp.float32)
    y = xf * lax.rsqrt(jnp.mean(xf * xf, axis=-1, keepdims=True) + EPS)
    return (y * g.astype(jnp.float32)).astype(x.dtype)

def _causal_dwconv(x, w, b):
    k_width, chans = w.shape
    y = lax.conv_general_dilated(
        x, w[:, None, :].astype(x.dtype), window_strides=(1,),
        padding=[(k_width - 1, 0)], dimension_numbers=('NWC', 'WIO', 'NWC'),
        feature_group_count=chans)
    return y + b.astype(x.dtype)

def _split_heads(t, n_heads):
    b, s, _ = t.shape
    return t.reshape(b, s, n_heads, -1).transpose(0, 2, 1, 3)

def _merge_heads(t):
    b, h, s, d = t.shape
    return t.transpose(0, 2, 1, 3).reshape(b, s, h * d)

def _stick_breaking_attention(q, k, v):
    seq, dh = q.shape[2], q.shape[3]
    scale = 1.0 / math.sqrt(dh)
    q_pos = jnp.arange(Q_BLOCK)
    outs = []
    for blk in range(seq // Q_BLOCK):
        t0 = blk * Q_BLOCK
        t1 = t0 + Q_BLOCK
        z = jnp.einsum('bhtd,bhsd->bhts', q[:, :, t0:t1], k[:, :, :t1]).astype(jnp.float32) * scale
        strict = jnp.arange(t1)[None, :] < (t0 + q_pos)[:, None]
        log_fail = jnp.where(strict, jax.nn.log_sigmoid(-z), 0.0)
        log_after = lax.cumsum(log_fail, axis=3, reverse=True) - log_fail
        w = jnp.where(strict, jnp.exp(jax.nn.log_sigmoid(z) + log_after), 0.0)
        outs.append(jnp.einsum('bhts,bhsd->bhtd', w.astype(v.dtype), v[:, :, :t1]))
    return jnp.concatenate(outs, axis=2)

def _mlstm_chunkwise(q, k, v, i_pre, f_pre):
    bsz, nh, seq, dh = q.shape
    n_chunks = seq // ML_CHUNK
    k = k * (1.0 / math.sqrt(dh))

    def chunked(t):
        t = t.reshape(bsz, nh, n_chunks, ML_CHUNK, *t.shape[3:])
        return jnp.moveaxis(t, 2, 0)

    log_f = jax.nn.log_sigmoid(f_pre)
    causal = jnp.tril(jnp.ones((ML_CHUNK, ML_CHUNK), dtype=bool))

    def step(carry, inp):
        c_st, n_st, m_st = carry
        qc, kc, vc, ic, lfc = inp
        b = jnp.cumsum(lfc, axis=-1)
        log_d = jnp.where(causal, b[..., :, None] - b[..., None, :] + ic[..., None, :], -jnp.inf)
        m_inter = b + m_st[..., None]
        m_t = jnp.maximum(m_inter, jnp.max(log_d, axis=-1))
        s = jnp.einsum('bhtd,bhsd->bhts', qc, kc) * jnp.exp(log_d - m_t[..., None])
        w_inter = jnp.exp(m_inter - m_t)
        num = (jnp.einsum('bhts,bhsd->bhtd', s, vc)
               + w_inter[..., None] * jnp.einsum('bhvk,bhtk->bhtv', c_st, qc))
        den = jnp.sum(s, axis=-1) + w_inter * jnp.einsum('bhk,bhtk->bht', n_st, qc)
        h = num / jnp.maximum(jnp.abs(den), jnp.exp(-m_t))[..., None]
        b_last = b[..., -1]
        log_g = b_last[..., None] - b + ic
        m_new = jnp.maximum(b_last + m_st, jnp.max(log_g, axis=-1))
        decay = jnp.exp(b_last + m_st - m_new)
        wk = jnp.exp(log_g - m_new[..., None])
        c_new = decay[..., None, None] * c_st + jnp.einsum('bhs,bhsv,bhsk->bhvk', wk, vc, kc)
        n_new = decay[..., None] * n_st + jnp.einsum('bhs,bhsk->bhk', wk, kc)
        return (c_new, n_new, m_new), h

    init = (jnp.zeros((bsz, nh, dh, dh), jnp.float32),
            jnp.zeros((bsz, nh, dh), jnp.float32),
            jnp.zeros((bsz, nh), jnp.float32))
    _, h = lax.scan(step, init, (chunked(q), chunked(k), chunked(v), chunked(i_pre), chunked(log_f)))
    return jnp.moveaxis(h, 0, 2).reshape(bsz, nh, seq, dh)

def _memory_cross_attention(q, mem_n, w_kv, g_q, g_k):
    k, v = jnp.split(mem_n @ w_kv, 2, axis=-1)
    qh = _rmsnorm(_split_heads(q, XA_HEADS), g_q)
    kh = _rmsnorm(_split_heads(k, XA_HEADS), g_k)
    vh = _split_heads(v, XA_HEADS)
    scores = jnp.einsum('bhsd,bhmd->bhsm', qh, kh).astype(jnp.float32) * (1.0 / math.sqrt(XA_HEAD_DIM))
    p = jax.nn.softmax(scores, axis=-1)
    return _merge_heads(jnp.einsum('bhsm,bhmd->bhsd', p.astype(vh.dtype), vh))

def second_inputs(seed: int = 0) -> dict:
    key = jax.random.key(seed)
    ks = jax.random.split(key, 24)

    def nrm(k, shape, scale):
        return jax.random.normal(k, shape, jnp.float32) * scale

    def gain(k, shape):
        return 1.0 + 0.02 * jax.random.normal(k, shape, jnp.float32)

    return {
        'x': nrm(ks[0], (BATCH, SEQ, D_MODEL), 1.0),
        'mem': nrm(ks[1], (BATCH, N_MEM, D_MODEL), 1.0),
        'g_mix': gain(ks[2], (DEPTH_2, D_MODEL)),
        'w_in': nrm(ks[3], (DEPTH_2, D_MODEL, IN_TOTAL), D_MODEL ** -0.5),
        'ml_conv_w': nrm(ks[4], (DEPTH_2, ML_CONV, 2 * ML_WIDTH), ML_CONV ** -0.5),
        'ml_conv_b': nrm(ks[5], (DEPTH_2, 2 * ML_WIDTH), 0.01),
        'ml_b_i': nrm(ks[6], (DEPTH_2, ML_HEADS), 0.1),
        'ml_b_f': jnp.linspace(3.0, 6.0, ML_HEADS, dtype=jnp.float32)[None, :] + nrm(ks[7], (DEPTH_2, ML_HEADS), 0.1),
        'ml_g_out': gain(ks[8], (DEPTH_2, ML_HEADS, ML_HEAD_DIM)),
        'g_mem': gain(ks[9], (DEPTH_2, D_MODEL)),
        'w_mem_kv': nrm(ks[10], (DEPTH_2, D_MODEL, 2 * XA_WIDTH), D_MODEL ** -0.5),
        'xa_g_q': gain(ks[11], (DEPTH_2, XA_HEAD_DIM)),
        'xa_g_k': gain(ks[12], (DEPTH_2, XA_HEAD_DIM)),
        'w_sb_out': nrm(ks[13], (DEPTH_2, SB_WIDTH, D_MODEL), SB_WIDTH ** -0.5),
        'w_ml_out': nrm(ks[14], (DEPTH_2, ML_WIDTH, D_MODEL), ML_WIDTH ** -0.5),
        'w_xa_out': nrm(ks[15], (DEPTH_2, XA_WIDTH, D_MODEL), XA_WIDTH ** -0.5),
        'w_o': nrm(ks[16], (DEPTH_2, D_MODEL, D_MODEL), D_MODEL ** -0.5),
        'g_ffn': gain(ks[17], (DEPTH_2, D_MODEL)),
        'w_up': nrm(ks[18], (DEPTH_2, D_MODEL, 2 * D_FF), D_MODEL ** -0.5),
        'ff_conv_w': nrm(ks[19], (DEPTH_2, FF_CONV, 2 * D_FF), FF_CONV ** -0.5),
        'ff_conv_b': nrm(ks[20], (DEPTH_2, 2 * D_FF), 0.01),
        'w_down': nrm(ks[21], (DEPTH_2, D_FF, D_MODEL), D_FF ** -0.5),
    }

def second_block(x, mem, g_mix, w_in, ml_conv_w, ml_conv_b, ml_b_i, ml_b_f, ml_g_out, g_mem,
              w_mem_kv, xa_g_q, xa_g_k, w_sb_out, w_ml_out, w_xa_out, w_o, g_ffn, w_up,
              ff_conv_w, ff_conv_b, w_down):
    bsz, seq, _ = x.shape
    offsets = np.cumsum(IN_SIZES)[:-1].tolist()
    for l in range(DEPTH_2):
        h = _rmsnorm(x, g_mix[l])
        (sb_q, sb_k, sb_v, ml_q, ml_k, ml_v, ml_o, ml_i, ml_f, xa_q, gate_pre) = jnp.split(
            h @ w_in[l], offsets, axis=-1)

        y_sb = _merge_heads(_stick_breaking_attention(
            _split_heads(sb_q, SB_HEADS), _split_heads(sb_k, SB_HEADS), _split_heads(sb_v, SB_HEADS)))

        ml_qk = jax.nn.silu(_causal_dwconv(jnp.concatenate([ml_q, ml_k], axis=-1), ml_conv_w[l], ml_conv_b[l]))
        ml_q, ml_k = jnp.split(ml_qk, 2, axis=-1)
        i_pre = (ml_i + ml_b_i[l]).astype(jnp.float32).transpose(0, 2, 1)
        f_pre = (ml_f + ml_b_f[l]).astype(jnp.float32).transpose(0, 2, 1)
        h_ml = _mlstm_chunkwise(
            _split_heads(ml_q, ML_HEADS).astype(jnp.float32),
            _split_heads(ml_k, ML_HEADS).astype(jnp.float32),
            _split_heads(ml_v, ML_HEADS).astype(jnp.float32), i_pre, f_pre)
        h_ml = _merge_heads(h_ml).astype(x.dtype).reshape(bsz, seq, ML_HEADS, ML_HEAD_DIM)
        h_ml = _rmsnorm(h_ml, ml_g_out[l]).reshape(bsz, seq, ML_WIDTH)
        y_ml = jax.nn.sigmoid(ml_o) * h_ml

        y_xa = _memory_cross_attention(xa_q, _rmsnorm(mem, g_mem[l]), w_mem_kv[l], xa_g_q[l], xa_g_k[l])

        gates = jax.nn.sigmoid(gate_pre).reshape(bsz, seq, N_BRANCH, D_MODEL)
        merged = (gates[:, :, 0] * (y_sb @ w_sb_out[l])
                  + gates[:, :, 1] * (y_ml @ w_ml_out[l])
                  + gates[:, :, 2] * (y_xa @ w_xa_out[l]))
        x = x + merged @ w_o[l]

        h = _rmsnorm(x, g_ffn[l])
        u = _causal_dwconv(h @ w_up[l], ff_conv_w[l], ff_conv_b[l])
        u_val, u_gate = jnp.split(u, 2, axis=-1)
        x = x + (jax.nn.silu(u_gate) * u_val) @ w_down[l]
    return x


def setup_inputs(seed=0):
    out = dict(first_inputs(seed))
    for name, value in second_inputs(seed + 1).items():
        if name != "x":
            out[name + "_2"] = value
    return out


def reference(
    x, positions, norm_w, final_norm_w, conv_w_in, conv_w_conv, conv_w_out, fox_w_in, fox_b_f,
    fox_w_out, gdn_w_in, gdn_w_conv, gdn_a_log, gdn_dt_bias, gdn_norm_w, gdn_w_out, swa_w_in,
    swa_sinks, swa_w_out, mem_2, g_mix_2, w_in_2, ml_conv_w_2, ml_conv_b_2, ml_b_i_2, ml_b_f_2,
    ml_g_out_2, g_mem_2, w_mem_kv_2, xa_g_q_2, xa_g_k_2, w_sb_out_2, w_ml_out_2, w_xa_out_2,
    w_o_2, g_ffn_2, w_up_2, ff_conv_w_2, ff_conv_b_2, w_down_2,
):
    x = first_block(
        x, positions, norm_w, final_norm_w, conv_w_in, conv_w_conv, conv_w_out, fox_w_in,
        fox_b_f, fox_w_out, gdn_w_in, gdn_w_conv, gdn_a_log, gdn_dt_bias, gdn_norm_w, gdn_w_out,
        swa_w_in, swa_sinks, swa_w_out,
    )
    return second_block(
        x, mem_2, g_mix_2, w_in_2, ml_conv_w_2, ml_conv_b_2, ml_b_i_2, ml_b_f_2, ml_g_out_2,
        g_mem_2, w_mem_kv_2, xa_g_q_2, xa_g_k_2, w_sb_out_2, w_ml_out_2, w_xa_out_2, w_o_2,
        g_ffn_2, w_up_2, ff_conv_w_2, ff_conv_b_2, w_down_2,
    )


_drawn_inputs = setup_inputs


def setup_inputs(seed=0):
    import zlib

    import numpy as np

    out = dict(_drawn_inputs(seed))
    spreads = {}
    factors = {'swa_sinks': 8.0,
     'g_mix_2': 4.313,
     'ml_conv_b_2': 64.0,
     'ml_b_i_2': 200.0,
     'ml_g_out_2': 34.358,
     'g_mem_2': 8.0,
     'xa_g_q_2': 8.0,
     'xa_g_k_2': 8.0,
     'g_ffn_2': 13.55,
     'ff_conv_b_2': 27.482}
    for name, (base, spread) in spreads.items():
        noise = np.random.default_rng([zlib.crc32(name.encode()), seed]).standard_normal(out[name].shape)
        drawn = base * np.exp(spread * noise) if base else spread * noise
        out[name] = __import__('jax').numpy.asarray(drawn.astype(out[name].dtype))
    for name, factor in factors.items():
        out[name] = (out[name] * factor).astype(out[name].dtype)
    return out
```

```python
from contextlib import ExitStack

import numpy as np
import concourse.bass as bass
from concourse import mybir

P = 128
T = 512
D = 1024
NT = T // P
ND = D // P
MEM = 256
FOX_H = GDN_H = 8
ML_H = XA_H = 4
SWA_H, SWA_KV = 16, 4
SB_H = 8
HD = 64
FF = 2816
NF = FF // P
EPS = 1e-6
NEG = -1e30
KU = 8
RAW, SPLIT, BANKS = 3, 3, 3



def stream():
    units, tiles = [], {}

    def tile(weight, i, kc, cols, operand, tokens=T, k0=0, tag=None):
        tiles[tag or (weight, i)] = len(tiles)
        for k in range(0, kc, KU):
            n = min(KU, kc - k)
            units.append((weight, i, k0 + k, n, cols, operand, tokens, k == 0, k + n == kc, len(tiles) - 1))

    def residual(weight):
        for i in range(ND):
            tile(weight, i, ND, P, "y")

    for j in range(ND):
        for part in (1, 2, 0, 3):
            tile("conv_w_in", part * ND + j, ND, P, "xw0")
    residual("conv_w_out")
    tile("fox_w_f", 0, ND, FOX_H, "xw1")
    for h in range(FOX_H):
        for part in range(4):
            tile("fox_w_in", part * FOX_H + h, ND, P, "xw1")
    residual("fox_w_out")
    tile("gdn_w_beta", 0, ND, GDN_H, "xw2")
    tile("gdn_w_a", 0, ND, GDN_H, "xw2")
    for h in range(GDN_H):
        for part in range(4):
            tile("gdn_w_in", part * GDN_H + h, ND, P, "xw2")
    residual("gdn_w_out")
    for i in (8, 9, 10, 11):
        tile("swa_w_in", i, ND, P, "xw3")
    for j in range(ND):
        tile("swa_w_in", j, ND, P, "xw3")
        tile("swa_w_in", 12 + j, ND, P, "xw3")
    residual("swa_w_out")
    for i in range(ND):
        tile("w_mem_kv_2", i, ND, P, "mem", MEM)
    tile("ml_w_i", 0, ND, ML_H, "xw4")
    tile("ml_w_f", 0, ND, ML_H, "xw4")
    for h in range(ML_H):
        for part in range(4):
            tile("w_ml", part * ML_H + h, ND, P, "xw4")
    for j in range(SB_H // 2):
        for part in range(3):
            tile("w_sb", part * 4 + j, ND, P, "xw4")
    for h in range(XA_H):
        tile("w_xa", h, ND, P, "xw4")
    for b, w in enumerate(("w_sb_out_2", "w_ml_out_2", "w_xa_out_2")):
        for m in range(ND):
            tile("w_gate", b * ND + m, ND, P, "xw4")
            tile(w, m, 4, P, w)
    for m in range(ND):
        tile("w_o_2", m, ND, P, "merged")
    groups = [(0, 8), (8, 16), (16, NF)]
    for g, (a, b) in enumerate(groups):
        for j in range(a, b):
            tile("w_up_2", j, ND, P, "xw5")
            tile("w_up_2", NF + j, ND, P, "xw5")
            if g and j == a:
                for m in range(ND):
                    tile("w_down_2", m, KU, P, "u", k0=groups[g - 1][0], tag=("down", g - 1, m))
    for m in range(ND):
        tile("w_down_2", m, NF - 16, P, "u", k0=16, tag=("down", 2, m))
    return units, tiles


UNITS, TILES = stream()
LAST_UNIT = {u[9]: n for n, u in enumerate(UNITS)}
WEIGHTS = {u[0]: None for u in UNITS}

COL_NAMES = [("norm_w", 4 * ND), ("final_norm_w", ND), ("g_mix_2", ND), ("g_mem_2", ND), ("g_ffn_2", ND),
             ("conv_w_conv", 3 * ND), ("gdn_w_conv", 4 * 3 * ND), ("gdn_norm_w", 1),
             ("ml_conv_w_2", 4 * ND), ("ml_conv_b_2", ND), ("ml_g_out_2", ML_H), ("xa_g_q_2", 1), ("xa_g_k_2", 1),
             ("ff_conv_w_2", 3 * 2 * NF), ("ff_conv_b_2", 2 * NF)]
COL = {}
for _n, _k in COL_NAMES:
    COL[_n] = sum(k for _, k in COL_NAMES[:len(COL)])
NCOL = sum(k for _, k in COL_NAMES)
ROW_NAMES = ["fox_b_f", "gdn_a_log", "gdn_dt_bias", "ml_b_i_2", "ml_b_f_2"]
MATS = ["ident", "ones", "mean_d", "mean_h", "upper_incl", "upper", "neg_lower_incl", "neg_ones",
        "causal_add", "window_add", "rot"] + [f"dup{g}" for g in range(2)] + [f"duprot{g}" for g in range(2)] \
    + ["level0"] + [f"lower{l}" for l in range(1, 7)]
MAT = {n: i for i, n in enumerate(MATS)}


def constants():
    p, f = np.arange(P)[:, None], np.arange(P)[None, :]
    m = {"ident": p == f, "ones": p >= 0 * f, "mean_d": (p >= 0 * f) / D, "mean_h": (p >= 0 * f) / P,
         "upper_incl": f >= p, "upper": f > p, "neg_lower_incl": -1.0 * (f <= p), "neg_ones": -1.0 * (p >= 0 * f),
         "causal_add": np.where(f <= p, 0, NEG), "window_add": np.where(f > p, 0, NEG)}
    half = HD // 2
    rot = np.zeros((P, P))
    for o in range(P):
        lo = o % HD < half
        rot[o + half if lo else o - half, o] = -1.0 if lo else 1.0
    m["rot"] = rot
    for g in range(2):
        dup = 1.0 * (p == g * HD + f % HD)
        m[f"dup{g}"], m[f"duprot{g}"] = dup, dup @ rot
    for l in range(7):
        s = 1 << l
        pair = (p // (2 * s) == f // (2 * s)) & (p % (2 * s) < s) & (f % (2 * s) >= s)
        if l:
            m[f"lower{l}"] = pair.T
        else:
            m["level0"] = pair
    return np.ascontiguousarray(np.stack([m[n].astype(np.float32) for n in MATS], axis=1).reshape(P, -1))


def inv_freq():
    half = HD // 2
    freq = (np.float32(10000.0) ** (-np.arange(half, dtype=np.float32) / np.float32(half))).astype(np.float32)
    return np.ascontiguousarray(freq[np.arange(P) % half][:, None])


def block_program(nc, a, out):
    f32, f32r, i32 = mybir.dt.float32, mybir.dt.float32r, mybir.dt.int32
    ALU, ACT, AX = mybir.AluOpType, mybir.ActivationFunctionType, mybir.AxisListType
    mult, add, sub, mx, mn = ALU.mult, ALU.add, ALU.subtract, ALU.max, ALU.min
    with ExitStack() as ctx:
        def sb(name, shape, dt=f32):
            return ctx.enter_context(nc.sbuf_tensor(name, shape, dt))

        sems = {}

        def s(name):
            if name not in sems:
                sems[name] = ctx.enter_context(nc.semaphore(name))
            return sems[name]

        x = sb("x", [P, ND, T])
        xw_hi, xw_lo = sb("xw_hi", [P, ND, T], f32r), sb("xw_lo", [P, ND, T], f32r)
        y_hi, y_lo = sb("y_hi", [P, 12, T], f32r), sb("y_lo", [P, 12, T], f32r)
        raw = sb("raw", [P, RAW, KU * P])
        w_hi, w_lo = sb("w_hi", [P, SPLIT, KU * P], f32r), sb("w_lo", [P, SPLIT, KU * P], f32r)
        rstd = sb("rstd", [P, T])
        cols, mats = sb("cols", [P, NCOL]), sb("mats", [P, len(MATS), P])
        rows = sb("rows", [8, len(ROW_NAMES)])
        freq, sinks = sb("freq", [P, 1]), sb("sinks", [P, SWA_H])
        v_tmp, sq = sb("v_tmp", [P, T]), sb("sq", [P, 3, T])
        ARENA = 12560
        arena = sb("arena", [P, ARENA])
        ps_lin = ctx.enter_context(nc.psum_tensor("ps_lin", [P, BANKS, T], f32))
        ps_att = ctx.enter_context(nc.psum_tensor("ps_att", [P, 4, T], f32))
        ps_aux = ctx.enter_context(nc.psum_tensor("ps_aux", [P, T], f32))
        operands = {"y": (y_hi, y_lo), "merged": (xw_hi, xw_lo), "u": (y_hi, y_lo)}

        def carve():
            at = [0]

            def take(*shape):
                n = int(np.prod(shape))
                view = arena[:, at[0]:at[0] + n]
                at[0] += n
                assert at[0] <= ARENA, at[0]
                if len(shape) == 2:
                    view = view.rearrange("p (a b) -> p a b", a=shape[0])
                if len(shape) == 3:
                    view = view.rearrange("p (a b c) -> p a b c", a=shape[0], b=shape[1])
                return view
            return take

        def mat(name):
            return mats[:, MAT[name], :]

        def col(name, i=0, n=P):
            return cols[0:n, COL[name] + i:COL[name] + i + 1]

        def row(name, n):
            i = ROW_NAMES.index(name)
            return rows[0:n, i:i + 1]

        def blk(ap, i, n=1):
            return ap[:, i * P:(i + n) * P]


        FOX_HD = ML_HD = XA_HD = P
        GDN_SCALE = P ** -0.5
        SWA_BASE = [0, P, 0, 2 * P]
        MAGIC = 1.5 * 2.0 ** 23
        TWO_PI = [2 * np.pi, 6.28125, float(np.float32(0.0019350051879882812)), 2 * np.pi - 6.28125 - 0.0019350051879882812]
        PI_F = float(np.nextafter(np.float32(np.pi), np.float32(0)))
        rstd_mem = sb("rstd_mem", [P, MEM])

        OFF = [0, 512, 896, 1152]
        W4 = 1280
        A = carve()
        conv = dict(c=A(T), u=A(2 + T), t=A(T), b=A(T), z=A(T), s=A(T))
        A = carve()
        fox = dict(q=A(2, T), k=A(2, T), v=A(2, T), z=A(2, T), L=A(NT, T), PT=A(NT, T), cb=A(T), vt=A(NT, P),
                   c=A(T), ab=A(T), r1=A(T), ones=A(T), st=A(3, NT))
        A = carve()
        gdn = dict(q=A(2, T), k=A(2, T), v=A(2, T), z=A(2, T), kb=A(T), qd=A(T), DT=A(T), LT=A(T), LTm=A(T), X=A(T),
                   Tm=A(T), U=A(T), QK=A(T), G=A(T), eG=A(T), beta=A(T), g=A(T), u=A(3 + T), t=A(T), n=A(T),
                   S=A(P), cols=A(4, NT, 8), ea=A(1))
        gdn.update(be=gdn["kb"], el=gdn["qd"], r1=gdn["DT"], r2=gdn["LT"], r3=gdn["LTm"], ones=gdn["X"],
                   kbg=gdn["DT"], kd=gdn["LT"], vb=gdn["LTm"], nwT=gdn["X"], vn=gdn["Tm"])
        A = carve()
        swa = dict(k=A(4, T), vp=A(4, 2, NT * P), cos=A(T), sin=A(T), q=A(T), qr=A(T), z=A(2, T), L0=A(NT, 2 * P),
                   PT=A(2, 2 * NT - 1, P), st=A(8, NT), s2=v_tmp[:])
        swa["L"] = [swa["L0"], sq[:, 1:3, :].rearrange("p a (b c) -> p (a b) c", b=2)]
        A = carve()
        mk = A(2 * ND, MEM)
        memx = mk[:, ND:2 * ND, :]
        kv_end = 2 * ND * MEM
        mem_k, mem_v = mk[:, 0:XA_H, :], mk[:, XA_H:2 * XA_H, :]
        A = carve()
        A(2 * XA_H * MEM)
        ml = dict(q=A(2, T), k=A(2, T), v=A(T), o=A(2, T), u=A(3 + T), t=A(T), m=A(T), nm=A(T), M=A(T), em=A(T),
                  rn=A(T), den=A(T), t2=A(T), ST=A(W4), vt=A(NT, P), gc=A(NT, 4))
        ml.update(g=ml["t2"], ones=ml["rn"], r1=ml["den"])
        A = carve()
        A(2 * XA_H * MEM)
        sbk = dict(q=A(2, T), k=A(2, T), v=A(T), vp=A(2, NT, P))
        sbk["L"] = [A(W4), A(W4)]
        sbk["W"] = [A(W4), A(W4), A(W4), sq.rearrange("p a b -> p (a b)")[:, 0:W4]]
        sbk["qk"] = [sbk["q"], sbk["k"]]
        A = carve()
        A(2 * XA_H * MEM)
        xa = dict(q=A(4, T), L=A(NT, MEM), PT=A(2, T), n=A(T), st=A(3, NT))
        mg = dict(m=A(ND, T), sg=A(2, T), t=A(T))
        A = carve()
        ff = dict(v=A(2 + T), g=A(2 + T), tv=A(T), tg=A(2, T), s=A(2, T))
        A = carve()
        A(2 * XA_H * MEM)
        xf = A(ND, T)

        def tile_of(weight, i):
            return TILES[(weight, i)]

        def bank_read(t):
            return s(f"evacuated{t % BANKS}")

        def reads(t):
            return t // BANKS + 1

        NORM_COL = [("norm_w", 0), ("norm_w", ND), ("norm_w", 2 * ND), ("norm_w", 3 * ND), ("g_mix_2", 0), ("g_ffn_2", 0)]

        block = ctx.enter_context(nc.Block())

        @block.sync
        def _(sp):
            for m in range(ND):
                sp.dma_start(x[:, m, :], a["x"][m]).then_inc(s("x_in"), 16)
                if m == 0:
                    sp.dma_start(cols[:], a["cols"]).then_inc(s("cols_in"), 16)
                    sp.dma_start(mats[:].rearrange("p a b -> p (a b)"), a["mats"]).then_inc(s("mats_in"), 16)
            sp.dma_start(rows[:], a["rows"]).then_inc(s("small_in"), 16)
            sp.dma_start(freq[:], a["freq"]).then_inc(s("small_in"), 16)
            sp.dma_start(sinks[:], a["sinks"]).then_inc(s("small_in"), 16)
            sp.dma_start(memx.rearrange("p a b -> p (a b)"), a["mem"]).then_inc(s("mem_in"), 16)
            for n, (w, i, k0, kc, c, _, _, _, _, t) in enumerate(UNITS):
                if n >= RAW:
                    sp.wait_ge(s("w_split"), 2 * (n - RAW + 1))
                sp.dma_start(raw[:, n % RAW, 0:kc * c], a[w][i][:, k0 * c:(k0 + kc) * c]).then_inc(s(f"w_raw{n % RAW}"), 16)
            for m in range(ND):
                sp.wait_ge(bank_read(TILES[("down", 2, m)]), reads(TILES[("down", 2, m)]))
                sp.dma_start(out[m], x[:, m, :]).then_inc(s("stored"), 16)
            sp.wait_ge(s("stored"), 16 * ND)

        @block.gpsimd
        def _(pool):
            for n, (w, i, k0, kc, c, _, _, _, _, t) in enumerate(UNITS):
                pool.wait_ge(s(f"w_raw{n % RAW}"), 16 * (n // RAW + 1))
                if n >= SPLIT:
                    pool.wait_ge(s("unit_done"), n - SPLIT + 1)
                r, h, l = raw[:, n % RAW, 0:kc * c], w_hi[:, n % SPLIT, 0:kc * c], w_lo[:, n % SPLIT, 0:kc * c]
                pool.tensor_scalar(h, r, 1.0, 0.0, mult, add).then_inc(s("w_split"), 1)
                pool.wait_ge(s("w_split"), 2 * n + 1)
                pool.tensor_tensor(l, r, h.bitcast(f32), sub).then_inc(s("w_split"), 1)

        @block.vector
        def _(dve):
            count = {}

            def made(name):
                count[name] = count.get(name, 0) + 1
                return count[name]

            def step(ins):
                ins.then_inc(s("dve_step"), 1)
                dve.wait_ge(s("dve_step"), made("dve_step"))

            def tt(o, p, q, op):
                return dve.tensor_tensor(o, p, q, op)

            def ts(o, p, a1, op0, a2=None, op1=None):
                return dve.tensor_scalar(o, p, a1, a2, op0, op1) if op1 else dve.tensor_scalar(o, p, a1, None, op0)

            def stt(o, p, sc, q, op0, op1):
                return dve.scalar_tensor_tensor(o, p, sc, q, op0, op1)

            def take(t):
                dve.wait_ge(s("unit_done"), LAST_UNIT[t] + 1)
                return ps_lin[:, t % BANKS, :], f"evacuated{t % BANKS}"

            def evac(t, dst, n=P, tokens=T, scale=None):
                ps, freed = take(t)
                tt(dst, ps[0:n, 0:tokens], (rstd if scale is None else scale)[0:n, 0:tokens], mult).then_inc(s(freed), 1)
                dve.wait_ge(s(freed), made(freed))

            def split(src, hi, lo, ready):
                step(dve.tensor_copy(hi, src))
                tt(lo, src, hi.bitcast(f32), sub).then_inc(s(ready), 1)
                dve.wait_ge(s(ready), made(ready))

            def normed(m, norm):
                name, base = NORM_COL[norm]
                ts(v_tmp[:], x[:, m, :], col(name, base + m), mult).then_inc(s("x_ready"), 1)
                dve.wait_ge(s("x_ready"), made("x_ready"))
                split(v_tmp[:], xw_hi[:, m, :], xw_lo[:, m, :], "xw_ready")

            def add_square(k, m):
                if m:
                    dve.wait_ge(s("sq_ready"), ND * k + m + 1)
                    tt(sq[:, 0, :], sq[:, 0, :], sq[:, 1 + m % 2, :], add).then_inc(s("sq_added"), 1)
                    dve.wait_ge(s("sq_added"), made("sq_added"))

            def residual(tiles, norm):
                for m in range(ND):
                    ps, freed = take(tiles[m])
                    tt(x[:, m, :], x[:, m, :], ps, add).then_inc(s(freed), 1)
                    dve.wait_ge(s(freed), made(freed))
                    if norm is not None:
                        normed(m, norm)
                    if m and norm is not None:
                        add_square(norm if norm < 4 else 6, m - 1)
                add_square(norm if norm < 4 else 6, ND - 1)

            def conv_taps(t, u, taps, weight, stride, j, bias=None, signal=None):
                back = taps - 1
                if bias is None:
                    step(ts(t, u[:, back:back + T], col(weight, back * stride + j), mult))
                else:
                    step(ts(t, u[:, back:back + T], col(weight, back * stride + j), mult, bias, add))
                for k in range(back):
                    tap = stt(t, u[:, k:k + T], col(weight, k * stride + j), t, mult, add)
                    if k == back - 1 and signal:
                        tap.then_inc(s(signal), 1)
                        dve.wait_ge(s(signal), made(signal))
                    else:
                        step(tap)

            dve.wait_ge(s("cols_in"), 16)
            dve.wait_ge(s("x_in"), 16 * ND)
            for m in range(ND):
                normed(m, 0)
                add_square(0, m)
            dve.wait_ge(s("mem_in"), 16)
            for m in range(1, ND):
                dve.wait_ge(s("mem_sq"), m + 1)
                tt(sq[:, 0, 0:MEM], sq[:, 0, 0:MEM], sq[:, 1 + m % 2, 0:MEM], add).then_inc(s("mem_added"), 1)
                dve.wait_ge(s("mem_added"), m)
            memv = y_hi[:, 8:12, :].rearrange("p a (c t) -> p (a c) t", t=MEM), y_lo[:, 8:12, :].rearrange("p a (c t) -> p (a c) t", t=MEM)
            for m in range(ND):
                step(ts(v_tmp[:, 0:MEM], memx[:, m, :], col("g_mem_2", m), mult))
                split(v_tmp[:, 0:MEM], memv[0][:, m, :], memv[1][:, m, :], "mem_ready")

            dve.wait_ge(s("mem_sq"), ND)
            step(dve.memset(conv["u"][:, 0:2], 0.0))
            dve.wait_ge(s("rstd_ready"), 1)
            for j in range(ND):
                c_t, v_t, b_t, z_t = (tile_of("conv_w_in", part * ND + j) for part in (1, 2, 0, 3))
                evac(c_t, conv["c"])
                evac(v_t, conv["u"][:, 2:2 + T])
                step(tt(conv["u"][:, 2:2 + T], conv["u"][:, 2:2 + T], conv["c"], mult))
                conv_taps(conv["t"], conv["u"], 3, "conv_w_conv", ND, j)
                evac(b_t, conv["b"])
                step(tt(conv["t"], conv["t"], conv["b"], mult))
                evac(z_t, conv["z"])
                dve.wait_ge(s("z_silu"), j + 1)
                step(tt(v_tmp[:], conv["t"], conv["s"], mult))
                split(v_tmp[:], y_hi[:, j, :], y_lo[:, j, :], "y_ready")
            residual([tile_of("conv_w_out", m) for m in range(ND)], 1)

            dve.wait_ge(s("rstd_ready"), 2)
            F = fox
            step(dve.memset(F["ones"][0:8, :], 1.0))
            evac(tile_of("fox_w_f", 0), F["r1"][0:8, :], n=FOX_H)
            dve.wait_ge(s("small_in"), 48)
            ts(F["r1"][0:8, :], F["r1"][0:8, :], row("fox_b_f", 8), add).then_inc(s("softplus_in"), 1)
            dve.wait_ge(s("softplus_in"), made("softplus_in"))
            dve.wait_ge(s("softplus_out"), 1)
            step(stt(F["r1"][0:8, :], F["r1"][0:8, :], 0.0, F["ab"][0:8, :], mn, sub))
            dve.tensor_tensor_scan(F["c"][0:8, :], F["ones"][0:8, :], F["r1"][0:8, :], 0.0, mult, add).then_inc(s("fox_c"), 1)
            dve.wait_ge(s("fox_c"), made("fox_c"))
            for r in range(FOX_H + 1):
                h = r - 1
                if r < FOX_H:
                    evac(tile_of("fox_w_in", r), F["q"][:, r % 2, :])
                if h >= 0:
                    st = F["st"]
                    dve.wait_ge(s("fox_cb"), h + 1)
                    for i in range(NT):
                        n = (i + 1) * P
                        dve.wait_ge(s("fox_scores"), NT * h + i + 1)
                        stt(F["L"][:, i, 0:n], ps_att[:, i, 0:n], FOX_HD ** -0.5, F["cb"][:, 0:n], mult, sub).then_inc(s("fox_scored"), 1)
                        dve.wait_ge(s("fox_scored"), made("fox_scored"))
                        step(tt(blk(F["L"][:, i, :], i), blk(F["L"][:, i, :], i), mat("causal_add"), add))
                        step(dve.tensor_reduce(st[:, 0, i:i + 1], F["L"][:, i, 0:n], AX.X, mx))
                        ts(st[:, 0, i:i + 1], st[:, 0, i:i + 1], -1.0, mult).then_inc(s("fox_max"), 1)
                        dve.wait_ge(s("fox_max"), made("fox_max"))
                if r < FOX_H:
                    evac(tile_of("fox_w_in", 8 + r), F["k"][:, r % 2, :])
                if h >= 0:
                    for i in range(NT):
                        n = (i + 1) * P
                        dve.wait_ge(s("fox_exp"), NT * h + i + 1)
                        step(dve.reciprocal(st[:, 2, i:i + 1], st[:, 1, i:i + 1]))
                        ts(F["L"][:, i, 0:n], F["L"][:, i, 0:n], st[:, 2, i:i + 1], mult).then_inc(s("fox_p"), 1)
                        dve.wait_ge(s("fox_p"), made("fox_p"))
                if r < FOX_H:
                    evac(tile_of("fox_w_in", 16 + r), F["v"][:, r % 2, :])
                if h >= 0:
                    for j in range(0, NT, 2):
                        dve.wait_ge(s("fox_pt"), NT * h + j + 1)
                        dve.tensor_copy(F["PT"][:, j, j * P:], ps_att[:, j, j * P:]).then_inc(s("fox_pt_dve"), 1)
                        dve.wait_ge(s("fox_pt_dve"), made("fox_pt_dve"))
                if r < FOX_H:
                    evac(tile_of("fox_w_in", 24 + r), F["z"][:, r % 2, :])
                if h >= 0:
                    dve.wait_ge(s("fox_o"), h + 1)
                    dve.wait_ge(s("z_silu"), h + 9)
                    tt(v_tmp[:], ps_aux[:], F["z"][:, h % 2, :], mult).then_inc(s("head_out"), 1)
                    dve.wait_ge(s("head_out"), made("head_out"))
                    split(v_tmp[:], y_hi[:, h, :], y_lo[:, h, :], "y_ready")
            residual([tile_of("fox_w_out", m) for m in range(ND)], 2)

            dve.wait_ge(s("rstd_ready"), 3)
            F = gdn
            R8 = slice(0, 8)
            step(dve.memset(F["u"][:, 0:3], 0.0))
            step(dve.memset(F["ones"][R8, :], 1.0))
            evac(tile_of("gdn_w_beta", 0), F["r1"][R8, :], n=8)
            dve.wait_ge(s("gdn_tanh"), 1)
            step(ts(F["beta"][R8, :], F["r1"][R8, :], 0.5, mult, 0.5, add))
            evac(tile_of("gdn_w_a", 0), F["r2"][R8, :], n=8)
            ts(F["r2"][R8, :], F["r2"][R8, :], row("gdn_dt_bias", 8), add).then_inc(s("softplus_in"), 1)
            dve.wait_ge(s("softplus_in"), made("softplus_in"))
            dve.wait_ge(s("softplus_out"), 2)
            step(stt(F["r2"][R8, :], F["r2"][R8, :], 0.0, F["r3"][R8, :], mx, add))
            step(ts(F["r2"][R8, :], F["r2"][R8, :], F["ea"][R8, :], mult, -1.0, mult))
            for c in range(NT):
                dve.tensor_tensor_scan(blk(F["g"][R8, :], c), blk(F["ones"][R8, :], c), blk(F["r2"][R8, :], c), 0.0, mult, add).then_inc(s("gdn_cumsum"), 1)
                dve.wait_ge(s("gdn_cumsum"), made("gdn_cumsum"))
            dve.wait_ge(s("gdn_eg"), NT + 1)
            step(tt(F["be"][R8, :], F["r1"][R8, :], F["beta"][R8, :], mult))
            ts(F["r2"][R8, :], F["g"][R8, :], -1.0, mult).then_inc(s("rows_ready"), 1)
            dve.wait_ge(s("rows_ready"), made("rows_ready"))
            dve.wait_ge(s("rows_turned"), 1)
            dve.tensor_copy(F["cols"].rearrange("p a b c -> p (a b c)"), ps_aux[:, 0:4 * NT * 8]).then_inc(s("columns"), 1)
            dve.wait_ge(s("columns"), made("columns"))

            def gdn_tile(r, part):
                t = tile_of("gdn_w_in", part * 8 + r)
                dst = F["qkvz"[part]][:, r % 2, :]
                if part == 3:
                    evac(t, dst)
                    return
                n, j = 3 * r + part, part * 8 + r
                if n:
                    dve.wait_ge(s("gdn_conv"), n)
                evac(t, F["u"][:, 3:3 + T])
                if n:
                    dve.wait_ge(s("gdn_silu"), n)
                yield
                step(ts(F["t"], F["u"][:, 3:3 + T], col("gdn_w_conv", 3 * 24 + j), mult))
                step(stt(F["t"], F["u"][:, 0:T], col("gdn_w_conv", j), F["t"], mult, add))
                yield
                step(stt(F["t"], F["u"][:, 1:1 + T], col("gdn_w_conv", 24 + j), F["t"], mult, add))
                stt(F["t"], F["u"][:, 2:2 + T], col("gdn_w_conv", 2 * 24 + j), F["t"], mult, add).then_inc(s("gdn_conv"), 1)
                yield
                if part:
                    dve.wait_ge(s("gdn_rn"), 2 * r + part)
                    dst = F["qkv"[part - 1]][:, r % 2, :]
                    stt(dst, dst, GDN_SCALE if part == 1 else 1.0, F["n"], mult, mult).then_inc(s("gdn_qk"), 1)

            def gdn_head(h, fill):
                q_, k_, v_, z_ = (F[n][:, h % 2, :] for n in "qkvz")
                b4 = lambda ap: ap.rearrange("p (c t) -> p c t", c=NT)
                wide = lambda name: mat(name).unsqueeze(1).to_broadcast([P, NT, P])
                colb = lambda i: F["cols"][:, i, :, h:h + 1].to_broadcast([P, NT, P])
                fill(2)
                dve.wait_ge(s("gdn_bc"), 2 * h + 2)
                dve.wait_ge(s("gdn_qk"), 2 * h + 2)
                tt(F["kb"], k_, ps_att[:, 3, :], mult).then_inc(s("gdn_kb"), 1)
                dve.wait_ge(s("gdn_kb"), made("gdn_kb"))
                dve.wait_ge(s("gdn_bcG"), h + 1)
                step(tt(F["qd"], q_, F["eG"], mult))
                step(tt(b4(F["DT"]), b4(F["G"]), colb(3), add))
                ts(F["DT"], F["DT"], 0.0, mn).then_inc(s("gdn_diff"), 1)
                dve.wait_ge(s("gdn_diff"), made("gdn_diff"))
                fill(2)
                dve.wait_ge(s("gdn_A"), 2 * h + 1)
                dve.wait_ge(s("gdn_decay"), h + 1)
                step(tt(F["LT"], ps_att[:, 0, :], F["DT"], mult))
                step(tt(b4(F["LTm"]), b4(F["LT"]), wide("level0"), mult))
                for g in range(2):
                    half = slice(g * 2 * P, (g + 1) * 2 * P)
                    pair = lambda ap: ap[:, half].rearrange("p (c t) -> p c t", c=2)
                    tt(pair(F["U"]), mat("ident").unsqueeze(1).to_broadcast([P, 2, P]), pair(F["LTm"]), sub).then_inc(s("gdn_U"), 1)
                dve.wait_ge(s("gdn_A"), 2 * h + 2)
                tt(F["QK"], ps_att[:, 1, :], F["DT"], mult).then_inc(s("gdn_QK"), 1)
                dve.wait_ge(s("gdn_QK"), h + 1)
                step(tt(b4(F["QK"]), b4(F["QK"]), wide("upper_incl"), mult))
                if h:
                    gdn_out(h - 1)
                fill(1)
                for l in range(1, 7):
                    for g in range(2):
                        half = slice(g * 2 * P, (g + 1) * 2 * P)
                        pair = lambda ap: ap[:, half].rearrange("p (c t) -> p c t", c=2)
                        dve.wait_ge(s("gdn_XT"), 12 * h + 2 * l - 1 + g)
                        tt(pair(F["X"]), ps_att[:, 2 * g, 0:2 * P].rearrange("p (c t) -> p c t", c=2), mat(f"lower{l}").unsqueeze(1).to_broadcast([P, 2, P]), mult).then_inc(s("gdn_X"), 1)
                    fill(1)
                    for g in range(2):
                        half = slice(g * 2 * P, (g + 1) * 2 * P)
                        dve.wait_ge(s("gdn_XU"), 12 * h + 2 * l - 1 + g)
                        tt(F["U"][:, half], F["U"][:, half], ps_att[:, 2 * g + 1, 0:2 * P], sub).then_inc(s("gdn_U"), 1)
                    fill(2)
                fill(1)
                dve.wait_ge(s("gdn_tok"), h + 1)
                tt(b4(F["kbg"]), b4(ps_att[:, 0, :]), colb(1), mult).then_inc(s("gdn_kbg"), 1)
                dve.wait_ge(s("gdn_kbg"), made("gdn_kbg"))
                step(tt(b4(F["kd"]), b4(ps_att[:, 0, :]), colb(2), mult))
                tt(b4(F["vb"]), b4(ps_att[:, 3, :]), colb(0), mult).then_inc(s("gdn_vb"), 1)
                dve.wait_ge(s("gdn_vb"), made("gdn_vb"))
                fill(2)
                for c in range(NT):
                    dve.wait_ge(s("gdn_vn"), NT * h + c + 1)
                    dve.tensor_copy(blk(F["vn"], c), blk(ps_att[:, 1, :], c)).then_inc(s("gdn_vn_out"), 1)
                    dve.wait_ge(s("gdn_vn_out"), made("gdn_vn_out"))
                    if c < NT - 1:
                        dve.wait_ge(s("gdn_S"), (NT - 1) * h + c + 1)
                        if c == 0:
                            dve.tensor_copy(F["S"], ps_aux[:, 0:P]).then_inc(s("gdn_state"), 1)
                            dve.wait_ge(s("gdn_state"), made("gdn_state"))
                        else:
                            stt(F["S"], F["S"], F["eG"][:, (c + 1) * P - 1:(c + 1) * P], ps_aux[:, 0:P], mult, add).then_inc(s("gdn_state"), 1)
                            dve.wait_ge(s("gdn_state"), made("gdn_state"))
                    fill(1)
                dve.wait_ge(s("gdn_out"), h + 1)
                dve.tensor_copy(v_tmp[:], ps_att[:, 0, :]).then_inc(s("gdn_o"), 1)

            def gdn_out(h):
                dve.wait_ge(s("gdn_rno"), h + 1)
                dve.wait_ge(s("z_silu"), h + 17)
                stt(v_tmp[:], v_tmp[:], col("gdn_norm_w"), sq[:, 2, :], mult, mult).then_inc(s("gdn_on"), 1)
                dve.wait_ge(s("gdn_on"), made("gdn_on"))
                step(tt(v_tmp[:], v_tmp[:], F["z"][:, h % 2, :], mult))
                split(v_tmp[:], y_hi[:, h, :], y_lo[:, h, :], "y_ready")

            pieces = iter(())
            for r in range(GDN_H + 1):
                done = 0

                def fill(n):
                    nonlocal done, pieces
                    if r < GDN_H:
                        for k in range(done, min(done + n, 4 * ND)):
                            if k % ND == ND - 1:
                                for _ in pieces:
                                    pass
                                pieces = gdn_tile(r, k // ND)
                    done += n
                    next(pieces, None)
                if r:
                    gdn_head(r - 1, fill)
                while done < 4 * ND:
                    fill(1)
                for _ in pieces:
                    pass
            gdn_out(GDN_H - 1)
            residual([tile_of("gdn_w_out", m) for m in range(ND)], 3)

            F = swa
            dve.wait_ge(s("rstd_ready"), 4)
            dve.wait_ge(s("pos_in"), 16)
            pos, ang, kk, rr = F["q"], F["qr"], F["s2"], F["sin"]
            step(dve.tensor_copy(ang, pos.bitcast(i32)))
            step(ts(ang, ang, freq[:], mult))
            step(ts(kk, ang, 1.0 / TWO_PI[0], mult, MAGIC, add))
            step(ts(kk, kk, -MAGIC, add))
            for part in TWO_PI[1:]:
                step(stt(ang, kk, -part, ang, mult, add))
            ts(rr, ang, PI_F, mn, -PI_F, mx).then_inc(s("swa_angle"), 1)
            dve.wait_ge(s("swa_angle"), made("swa_angle"))
            step(dve.memset(F["vp"].rearrange("p a b c -> p (a b c)"), 0.0))
            dve.wait_ge(s("swa_sin"), 2)
            for kt in range(2):
                evac(tile_of("swa_w_in", 8 + kt), F["q"], )
                for g in range(2):
                    dve.wait_ge(s("swa_kdup"), 2 * kt + g + 1)
                    step(tt(F["k"][:, 2 * kt + g, :], ps_att[:, 2 * g, :], F["cos"], mult))
                    step(tt(F["qr"], ps_att[:, 2 * g + 1, :], F["sin"], mult))
                    tt(F["k"][:, 2 * kt + g, :], F["k"][:, 2 * kt + g, :], F["qr"], add).then_inc(s("swa_k"), 1)
                    dve.wait_ge(s("swa_k"), made("swa_k"))
            for vt in range(2):
                evac(tile_of("swa_w_in", 10 + vt), F["q"])
                dve.wait_ge(s("swa_vT"), vt + 1)
                for g in range(2):
                    src = ps_aux[:].rearrange("p (b c) -> p b c", b=NT)[:, :, g * HD:(g + 1) * HD]
                    for half in range(2):
                        dst = F["vp"][:, 2 * vt + g, half, :].rearrange("p (b c) -> p b c", b=NT)
                        dve.tensor_copy(dst[:, :, half * HD:(half + 1) * HD], src).then_inc(s("swa_v"), 1)
                        dve.wait_ge(s("swa_v"), made("swa_v"))
            for half in range(2):
                step(dve.memset(F["L"][half][:, 0, 0:P], 0.0))

            def swa_rope(j):
                dve.wait_ge(s("swa_qrot"), j + 1)
                step(tt(F["q"], F["qr"], F["cos"], mult))
                step(tt(F["s2"], ps_aux[:], F["sin"], mult))
                tt(F["q"], F["q"], F["s2"], add).then_inc(s("swa_q"), 1)
                dve.wait_ge(s("swa_q"), made("swa_q"))

            def swa_out(j):
                dve.wait_ge(s("swa_o"), j + 1)
                dve.wait_ge(s("z_silu"), j + 25)
                tt(v_tmp[:], ps_aux[:], F["z"][:, j % 2, :], mult).then_inc(s("head_out"), 1)
                dve.wait_ge(s("head_out"), made("head_out"))
                split(v_tmp[:], y_hi[:, j, :], y_lo[:, j, :], "y_ready")

            evac(tile_of("swa_w_in", 0), F["qr"])
            swa_rope(0)
            evac(tile_of("swa_w_in", 12), F["z"][:, 0, :])
            for j in range(ND):
                for half in range(2):
                    n, L, st = 2 * j + half, F["L"][half], F["st"][:, 4 * half:4 * half + 4, :]
                    if j:
                        dve.wait_ge(s("swa_ptT"), 2 * (n - 1))
                    for i in range(NT):
                        dve.wait_ge(s("swa_scores"), 2 * n + i // 2 + 1)
                        ps, base = ps_att[:, 2 * half + i // 2, :], SWA_BASE[i]
                        if i:
                            stt(L[:, i, 0:P], ps[:, base:base + P], HD ** -0.5, mat("window_add"), mult, add)
                            base += P
                        last = stt(L[:, i, P:2 * P], ps[:, base:base + P], HD ** -0.5, mat("causal_add"), mult, add)
                    step(last)
                    dve.tensor_reduce(st[:, 0, 0:1], L[:, 0, P:], AX.X, mx)
                    step(dve.tensor_reduce(st[:, 0, 1:], L[:, 1:, :], AX.X, mx))
                    ts(st[:, 0, :], st[:, 0, :], sinks[:, n:n + 1], mx, -1.0, mult).then_inc(s("swa_max"), 1)
                    dve.wait_ge(s("swa_max"), made("swa_max"))
                if j:
                    swa_out(j - 1)
                if j < ND - 1:
                    evac(tile_of("swa_w_in", j + 1), F["qr"])
                for half in range(2):
                    n, L, st = 2 * j + half, F["L"][half], F["st"][:, 4 * half:4 * half + 4, :]
                    dve.wait_ge(s("swa_exp"), n + 1)
                    step(tt(st[:, 1, :], st[:, 1, :], st[:, 2, :], add))
                    step(dve.reciprocal(st[:, 3, :], st[:, 1, :]))
                    tt(L, L, st[:, 3, :].unsqueeze(2).to_broadcast([P, NT, 2 * P]), mult).then_inc(s("swa_p"), 1)
                    dve.wait_ge(s("swa_p"), made("swa_p"))
                    if j < ND - 1 and half == 0:
                        swa_rope(j + 1)
                if j < ND - 1:
                    evac(tile_of("swa_w_in", 13 + j), F["z"][:, (j + 1) % 2, :])
            swa_out(ND - 1)
            for m in range(ND):
                ps, freed = take(tile_of("swa_w_out", m))
                tt(x[:, m, :], x[:, m, :], ps, add).then_inc(s(freed), 1)
                dve.wait_ge(s(freed), made(freed))
                ts(xf[:, m, :], x[:, m, :], col("final_norm_w", m), mult).then_inc(s("x_ready"), 1)
                dve.wait_ge(s("x_ready"), made("x_ready"))
                if m:
                    add_square(4, m - 1)
            add_square(4, ND - 1)
            dve.wait_ge(s("rstd_mem"), 1)

            def memory(i):
                evac(tile_of("w_mem_kv_2", i), (mem_k if i < XA_H else mem_v)[:, i % XA_H, :], tokens=MEM, scale=rstd_mem)

            for i in range(BANKS):
                memory(i)
            dve.wait_ge(s("rstd_ready"), 5)
            for m in range(ND):
                step(tt(x[:, m, :], xf[:, m, :], rstd[:], mult))
                normed(m, 4)
                add_square(5, m)

            for i in range(BANKS, ND):
                memory(i)

            dve.wait_ge(s("rstd_ready"), 6)
            F = ml
            R4 = slice(0, 4)
            step(dve.memset(F["u"][:, 0:3], 0.0))
            step(dve.memset(F["ones"][R4, :], 1.0))
            evac(tile_of("ml_w_i", 0), F["g"][R4, :], n=ML_H)
            step(ts(F["g"][R4, :], F["g"][R4, :], row("ml_b_i_2", 4), add))
            evac(tile_of("ml_w_f", 0), F["r1"][R4, :], n=ML_H)
            ts(F["r1"][R4, :], F["r1"][R4, :], row("ml_b_f_2", 4), add).then_inc(s("softplus_in"), 1)
            dve.wait_ge(s("softplus_in"), made("softplus_in"))
            dve.wait_ge(s("softplus_out"), 3)
            step(stt(F["r1"][R4, :], F["r1"][R4, :], 0.0, F["em"][R4, :], mn, sub))
            step(dve.tensor_tensor_scan(F["m"][R4, :], F["ones"][R4, :], F["r1"][R4, :], 0.0, mult, add))
            step(tt(F["g"][R4, :], F["g"][R4, :], F["m"][R4, :], sub))
            step(dve.tensor_tensor_scan(F["M"][R4, :], F["g"][R4, :], F["g"][R4, :], 0.0, mx, mx))
            step(ts(F["nm"][R4, :], F["M"][R4, :], -1.0, mult))
            tt(F["m"][R4, :], F["nm"][R4, :], F["m"][R4, :], sub).then_inc(s("rows_ready"), 1)
            dve.wait_ge(s("rows_ready"), made("rows_ready"))
            dve.wait_ge(s("rows_turned"), 2)
            dve.tensor_copy(F["gc"].rearrange("p a b -> p (a b)"), ps_aux[:, 0:NT * 4]).then_inc(s("columns"), 1)
            dve.wait_ge(s("columns"), made("columns"))
            for g in range(2):
                kg = mem_k[:, 2 * g:2 * g + 2, :].rearrange("p a b -> p (a b)")
                dve.wait_ge(s("xa_krn"), g + 1)
                stt(kg, kg, col("xa_g_k_2"), F["ST"][:, g * T:(g + 1) * T], mult, mult).then_inc(s("xa_k"), 1)
                dve.wait_ge(s("xa_vT"), g + 1)
                dve.tensor_copy(mem_v[:, 2 * g:2 * g + 2, :].rearrange("p a b -> p (a b)"), ps_att[:, 2 + g, :]).then_inc(s("xa_v"), 1)
            dve.wait_ge(s("xa_k"), 2)
            for r in range(ML_H + 1):
                h = r - 1
                for part in range(4):
                    if h >= 0:
                        hh, rn, den = F["t2"], F["rn"], F["den"]
                        if part == 0:
                            dve.wait_ge(s("ml_M"), h + 1)
                            for j in range(NT):
                                ts(F["ST"][:, OFF[j]:OFF[j] + T - j * P], F["M"][:, j * P:], F["gc"][:, j, h:h + 1], add, 0.0, mn).then_inc(s("ml_diff"), 1)
                                dve.wait_ge(s("ml_diff"), made("ml_diff"))
                            for j in range(NT):
                                dve.wait_ge(s("ml_decay"), NT * h + j + 1)
                                dve.wait_ge(s("ml_scores"), NT * h + j + 1)
                                step(stt(F["ST"][:, OFF[j]:OFF[j] + T - j * P], ps_att[:, j, j * P:], ML_HD ** -0.5, F["ST"][:, OFF[j]:OFF[j] + T - j * P], mult, mult))
                                tt(F["ST"][:, OFF[j]:OFF[j] + P], F["ST"][:, OFF[j]:OFF[j] + P], mat("upper_incl"), mult).then_inc(s("ml_st"), 1)
                                dve.wait_ge(s("ml_st"), made("ml_st"))
                        if part == 2:
                            dve.wait_ge(s("ml_abs"), h + 1)
                            step(tt(den, den, F["em"], mx))
                            step(dve.reciprocal(den, den))
                            tt(hh, ps_att[:, 0, :], den, mult).then_inc(s("ml_h"), 1)
                            dve.wait_ge(s("ml_h"), made("ml_h"))
                        if part == 3:
                            dve.wait_ge(s("ml_rn"), h + 1)
                            dve.wait_ge(s("ml_tanh"), h + 1)
                            step(ts(hh, hh, col("ml_g_out_2", h), mult, 0.5, mult))
                            step(tt(hh, hh, rn, mult))
                            step(stt(v_tmp[:], F["o"][:, h % 2, :], 1.0, hh, add, mult))
                            split(v_tmp[:], y_hi[:, 4 + h, :], y_lo[:, 4 + h, :], "ml_y")
                    if r < ML_H:
                        t = tile_of("w_ml", part * ML_H + r)
                        if part < 2:
                            evac(t, F["u"][:, 3:3 + T])
                            if 2 * r + part:
                                dve.wait_ge(s("ml_silu"), 2 * r + part)
                            i = part * ML_H + r
                            conv_taps(F["t"], F["u"], 4, "ml_conv_w_2", ND, i, bias=col("ml_conv_b_2", i), signal="ml_conv")
                        elif part == 2:
                            if r:
                                dve.wait_ge(s("ml_vT"), r)
                            evac(t, F["v"])
                        else:
                            evac(t, F["o"][:, r % 2, :])

            F = sbk
            step(dve.memset(F["vp"].rearrange("p a b c -> p (a b c)"), 0.0))
            def sb_sums(n):
                W = F["W"][n % 4]
                dve.wait_ge(s("sb_log"), n + 1)
                step(stt(W, F["L"][n % 2], 0.0, W, mx, add))
                for b in range(NT):
                    d = W[:, OFF[b]:OFF[b] + P]
                    tt(d, d, mat("upper"), mult).then_inc(s("sb_sp"), 1)
                dve.wait_ge(s("sb_sp"), NT * (n + 1))

            def sb_log_weights(n):
                for b in range(NT):
                    d = F["L"][n % 2][:, OFF[b]:OFF[b] + T - b * P]
                    dve.wait_ge(s("sb_after"), NT * n + b + 1)
                    tt(d, d, ps_att[:, b, b * P:], add).then_inc(s("sb_logw"), 1)
                dve.wait_ge(s("sb_logw"), NT * (n + 1))

            def sb_mask(n):
                dve.wait_ge(s("sb_exp"), n + 1)
                for b in range(NT):
                    d = F["W"][n % 4][:, OFF[b]:OFF[b] + P]
                    tt(d, d, mat("upper"), mult).then_inc(s("sb_W"), 1)
                dve.wait_ge(s("sb_W"), NT * (n + 1))

            def sb_out(j):
                dve.wait_ge(s("sb_o"), j + 1)
                dve.tensor_copy(v_tmp[:], ps_aux[:]).then_inc(s("head_out"), 1)
                dve.wait_ge(s("head_out"), made("head_out"))
                split(v_tmp[:], y_hi[:, j, :], y_lo[:, j, :], "sb_y")

            def sb_tile(part, j):
                evac(tile_of("w_sb", part * 4 + j), F["v"] if part == 2 else F["qk"][part][:, j % 2, :])

            for part in range(3):
                sb_tile(part, 0)
            sb_sums(0)
            for n in range(SB_H):
                j, even = n // 2, n % 2 == 0
                more = j < SB_H // 2 - 1
                if more:
                    sb_tile(0 if even else 2, j + 1)
                if even:
                    if j:
                        sb_out(j - 1)
                    dve.wait_ge(s("sb_vT"), j + 1)
                    src = ps_aux[:].rearrange("p (b c) -> p b c", b=NT)
                    for half in range(2):
                        d = slice(half * HD, (half + 1) * HD)
                        dve.tensor_copy(F["vp"][:, half, :, d], src[:, :, d]).then_inc(s("sb_v"), 1)
                    dve.wait_ge(s("sb_v"), 2 * (j + 1))
                sb_log_weights(n)
                if n < SB_H - 1:
                    sb_sums(n + 1)
                if more and even:
                    sb_tile(1, j + 1)
                sb_mask(n)

            F = xa
            for h in range(XA_H - 1):
                evac(tile_of("w_xa", h), F["q"][:, h, :])

            F = sbk
            sb_out(SB_H // 2 - 1)
            F = xa
            evac(tile_of("w_xa", XA_H - 1), F["q"][:, XA_H - 1, :])
            BRANCHES = ("w_sb_out_2", "w_ml_out_2", "w_xa_out_2")

            def gate_in(n):
                evac(tile_of("w_gate", n), mg["sg"][:, n % 2, :])

            def gate_out(n):
                b, m = n // ND, n % ND
                dve.wait_ge(s("gate_tanh"), n + 1)
                ps, freed = take(tile_of(BRANCHES[b], m))
                dst = mg["m"][:, m, :] if b == 0 else mg["t"]
                stt(dst, mg["sg"][:, n % 2, :], 1.0, ps, add, mult).then_inc(s(freed), 1)
                dve.wait_ge(s(freed), made(freed))
                if b:
                    step(tt(mg["m"][:, m, :], mg["m"][:, m, :], mg["t"], add))

            def xa_norm_q(h):
                dve.wait_ge(s("xa_qrn"), h + 1)
                stt(F["q"][:, h, :], F["q"][:, h, :], col("xa_g_q_2"), F["n"], mult, mult).then_inc(s("xa_q"), 1)
                dve.wait_ge(s("xa_q"), made("xa_q"))

            xa_norm_q(0)
            for h in range(XA_H):
                st = F["st"]
                for g in range(2):
                    dve.wait_ge(s("xa_scores"), 2 * h + g + 1)
                    last = dve.tensor_reduce(st[:, 0, 2 * g:2 * g + 2], ps_att[:, g, :].rearrange("p (a b) -> p a b", a=2), AX.X, mx)
                step(last)
                ts(st[:, 0, :], st[:, 0, :], -(XA_HD ** -0.5), mult).then_inc(s("xa_max"), 1)
                dve.wait_ge(s("xa_max"), made("xa_max"))
                if h < XA_H - 1:
                    xa_norm_q(h + 1)
                gate_in(2 * h)
                dve.wait_ge(s("xa_exp"), h + 1)
                step(dve.reciprocal(st[:, 2, :], st[:, 1, :]))
                tt(F["L"], F["L"], st[:, 2, :].unsqueeze(2).to_broadcast([P, NT, MEM]), mult).then_inc(s("xa_p"), 1)
                dve.wait_ge(s("xa_p"), made("xa_p"))
                gate_out(2 * h)
                for b in range(2):
                    dve.wait_ge(s("xa_ptT"), 2 * h + b + 1)
                    dve.tensor_copy(F["PT"][:, b, :], ps_att[:, 2 + b, :]).then_inc(s("xa_pt"), 1)
                dve.wait_ge(s("xa_pt"), 2 * h + 2)
                gate_in(2 * h + 1)
                gate_out(2 * h + 1)
                dve.wait_ge(s("xa_o"), h + 1)
                dve.tensor_copy(v_tmp[:], ps_aux[:]).then_inc(s("head_out"), 1)
                dve.wait_ge(s("head_out"), made("head_out"))
                split(v_tmp[:], y_hi[:, 8 + h, :], y_lo[:, 8 + h, :], "xa_y")

            for n in range(2 * XA_H, 3 * ND):
                gate_in(n)
                gate_out(n)
                if n >= 2 * ND:
                    m = n - 2 * ND
                    step(ts(v_tmp[:], mg["m"][:, m, :], 0.5, mult))
                    split(v_tmp[:], y_hi[:, m, :], y_lo[:, m, :], "merged")
            residual([tile_of("w_o_2", m) for m in range(ND)], 5)

            F = ff
            step(dve.memset(F["v"][:, 0:2], 0.0))
            step(dve.memset(F["g"][:, 0:2], 0.0))
            dve.wait_ge(s("rstd_ready"), 7)

            def down(g):
                for m in range(ND):
                    ps, freed = take(TILES[("down", g, m)])
                    tt(x[:, m, :], x[:, m, :], ps, add).then_inc(s(freed), 1)
                    dve.wait_ge(s(freed), made(freed))

            for c in range(NF):
                evac(tile_of("w_up_2", c), F["v"][:, 2:2 + T])
                conv_taps(F["tv"], F["v"], 3, "ff_conv_w_2", 2 * NF, c, bias=col("ff_conv_b_2", c))
                evac(tile_of("w_up_2", NF + c), F["g"][:, 2:2 + T])
                conv_taps(F["tg"][:, c % 2, :], F["g"], 3, "ff_conv_w_2", 2 * NF, NF + c, bias=col("ff_conv_b_2", NF + c), signal="ff_gate")
                dve.wait_ge(s("ff_silu"), c + 1)
                step(tt(v_tmp[:], F["tv"], F["s"][:, c % 2, :], mult))
                split(v_tmp[:], y_hi[:, c % 12, :], y_lo[:, c % 12, :], "u_ready")
                if c in (8, 16):
                    down(c // 8 - 1)
            down(2)

        @block.scalar
        def _(act):
            count = {}

            def made(name):
                count[name] = count.get(name, 0) + 1
                return count[name]

            def step(ins):
                ins.then_inc(s("act_step"), 1)
                act.wait_ge(s("act_step"), made("act_step"))

            def root(o, i, signal):
                step(act.activation(o, i, ACT.Ln, bias=EPS))
                act.activation(o, o, ACT.Exp, scale=-0.5).then_inc(s(signal), 1)
                act.wait_ge(s(signal), made(signal))

            def square(k, m):
                if m == 0 and k:
                    act.wait_ge(s("ss_done"), k)
                if m > 2:
                    act.wait_ge(s("sq_added"), (ND - 1) * k + m - 2)
                act.activation(sq[:, 1 + m % 2 if m else 0, :], x[:, m, :], ACT.Square).then_inc(s("sq_ready"), 1)

            act.wait_ge(s("x_in"), 16 * ND)
            for m in range(ND):
                square(0, m)
            act.wait_ge(s("ss_done"), 1)
            root(rstd[:], ps_aux[:], "rstd_ready")
            act.wait_ge(s("mem_in"), 16)
            for m in range(ND):
                if m > 2:
                    act.wait_ge(s("mem_added"), m - 2)
                act.activation(sq[:, 1 + m % 2 if m else 0, 0:MEM], memx[:, m, :], ACT.Square).then_inc(s("mem_sq"), 1)
            act.wait_ge(s("mem_ss"), 1)
            root(rstd_mem[:], ps_aux[:, 0:MEM], "rstd_mem")

            norm_no = [1]

            def norm(tiles=None):
                k = norm_no[0]
                for m in range(ND):
                    if tiles:
                        act.wait_ge(bank_read(tiles[m]), reads(tiles[m]))
                    else:
                        act.wait_ge(s("x_ready"), ND * k + m + 1)
                    square(k, m)
                act.wait_ge(s("ss_done"), k + 1)
                root(rstd[:], ps_aux[:], "rstd_ready")
                norm_no[0] += 1

            for j in range(ND):
                act.wait_ge(bank_read(tile_of("conv_w_in", 3 * ND + j)), reads(tile_of("conv_w_in", 3 * ND + j)))
                if j:
                    act.wait_ge(s("y_ready"), j)
                act.activation(conv["s"], conv["z"], ACT.Silu).then_inc(s("z_silu"), 1)
                act.wait_ge(s("z_silu"), made("z_silu"))
            norm([tile_of("conv_w_out", m) for m in range(ND)])

            F = fox
            act.wait_ge(s("softplus_in"), 1)
            step(act.activation(F["ab"][0:8, :], F["r1"][0:8, :], ACT.Abs))
            step(act.activation(F["ab"][0:8, :], F["ab"][0:8, :], ACT.Exp, scale=-1.0))
            act.activation(F["ab"][0:8, :], F["ab"][0:8, :], ACT.Ln, bias=1.0).then_inc(s("softplus_out"), 1)
            act.wait_ge(s("softplus_out"), made("softplus_out"))
            for r in range(FOX_H + 1):
                h = r - 1
                st = F["st"]
                if h >= 0:
                    act.wait_ge(s("fox_bc"), h + 1)
                    act.activation(F["cb"], ps_aux[:], ACT.Copy).then_inc(s("fox_cb"), 1)
                    act.wait_ge(s("fox_cb"), made("fox_cb"))
                    for i in range(NT):
                        n = (i + 1) * P
                        act.wait_ge(s("fox_max"), NT * h + i + 1)
                        act.activation(F["L"][:, i, 0:n], F["L"][:, i, 0:n], ACT.Exp, bias=st[:, 0, i:i + 1], accum_out=st[:, 1, i:i + 1]).then_inc(s("fox_exp"), 1)
                        act.wait_ge(s("fox_exp"), made("fox_exp"))
                    act.wait_ge(s("fox_vT"), h + 1)
                    act.activation(F["vt"].rearrange("p a b -> p (a b)"), ps_aux[:], ACT.Copy).then_inc(s("fox_v"), 1)
                    act.wait_ge(s("fox_v"), made("fox_v"))
                    for j in range(1, NT, 2):
                        act.wait_ge(s("fox_pt"), NT * h + j + 1)
                        act.activation(F["PT"][:, j, j * P:], ps_att[:, j, j * P:], ACT.Copy).then_inc(s("fox_pt_act"), 1)
                        act.wait_ge(s("fox_pt_act"), made("fox_pt_act"))
                if r < FOX_H:
                    act.wait_ge(bank_read(tile_of("fox_w_in", 24 + r)), reads(tile_of("fox_w_in", 24 + r)))
                    act.activation(F["z"][:, r % 2, :], F["z"][:, r % 2, :], ACT.Silu).then_inc(s("z_silu"), 1)
                    act.wait_ge(s("z_silu"), made("z_silu"))
            norm([tile_of("fox_w_out", m) for m in range(ND)])

            F = gdn
            R8 = slice(0, 8)
            act.wait_ge(bank_read(tile_of("gdn_w_beta", 0)), reads(tile_of("gdn_w_beta", 0)))
            act.activation(F["r1"][R8, :], F["r1"][R8, :], ACT.Tanh, scale=0.5).then_inc(s("gdn_tanh"), 1)
            act.wait_ge(s("gdn_tanh"), made("gdn_tanh"))
            act.wait_ge(s("small_in"), 48)
            step(act.activation(F["ea"][R8, :], row("gdn_a_log", 8), ACT.Exp))
            act.wait_ge(s("softplus_in"), 2)
            step(act.activation(F["r3"][R8, :], F["r2"][R8, :], ACT.Abs))
            step(act.activation(F["r3"][R8, :], F["r3"][R8, :], ACT.Exp, scale=-1.0))
            act.activation(F["r3"][R8, :], F["r3"][R8, :], ACT.Ln, bias=1.0).then_inc(s("softplus_out"), 1)
            act.wait_ge(s("softplus_out"), made("softplus_out"))
            act.wait_ge(s("gdn_cumsum"), NT)
            act.activation(F["r1"][R8, :], F["g"][R8, :], ACT.Exp).then_inc(s("gdn_eg"), 1)
            act.wait_ge(s("gdn_eg"), made("gdn_eg"))
            for c in range(NT):
                act.activation(blk(F["el"][R8, :], c), blk(F["g"][R8, :], c), ACT.Exp, scale=-1.0, bias=F["g"][R8, (c + 1) * P - 1:(c + 1) * P]).then_inc(s("gdn_eg"), 1)
                act.wait_ge(s("gdn_eg"), made("gdn_eg"))

            def gdn_tile(r, part):
                t = tile_of("gdn_w_in", part * 8 + r)
                dst = F["qkvz"[part]][:, r % 2, :]
                if part == 3:
                    yield
                    act.wait_ge(bank_read(t), reads(t))
                    act.activation(dst, dst, ACT.Silu).then_inc(s("z_silu"), 1)
                    return
                if part:
                    act.wait_ge(s("gdn_ss"), 2 * r + part)
                    if 2 * r + part > 1:
                        act.wait_ge(s("gdn_qk"), 2 * r + part - 1)
                    root(F["n"], ps_aux[:], "gdn_rn")
                yield
                yield
                yield
                act.wait_ge(s("gdn_conv"), 3 * r + part + 1)
                act.activation(dst, F["t"], ACT.Silu).then_inc(s("gdn_silu"), 1)
                if part < 2:
                    act.wait_ge(s("gdn_silu"), 3 * r + part + 1)
                    act.activation(sq[:, 1, :], dst, ACT.Square).then_inc(s("gdn_sq"), 1)

            def gdn_head(h, fill):
                fill(2)
                act.wait_ge(s("gdn_bc"), 2 * h + 1)
                step(act.activation(F["G"], ps_att[:, 2, :], ACT.Copy))
                act.activation(F["eG"], ps_att[:, 2, :], ACT.Exp).then_inc(s("gdn_bcG"), 1)
                act.wait_ge(s("gdn_bcG"), made("gdn_bcG"))
                if h:
                    gdn_rms(h - 1)
                act.wait_ge(s("gdn_diff"), h + 1)
                act.activation(F["DT"], F["DT"], ACT.Exp).then_inc(s("gdn_decay"), 1)
                act.wait_ge(s("gdn_decay"), made("gdn_decay"))
                fill(2)
                for l in range(6):
                    for g in range(2):
                        half = slice(g * 2 * P, (g + 1) * 2 * P)
                        act.wait_ge(s("gdn_UT"), 12 * h + 2 * l + g + 1)
                        act.activation(F["Tm"][:, half], ps_att[:, 2 * g, 0:2 * P], ACT.Copy).then_inc(s("gdn_T"), 1)
                    if l == 0:
                        fill(1)
                    fill(1)
                    fill(2)
                fill(1)
                act.wait_ge(s("gdn_w"), h + 1)
                act.activation(F["nwT"], ps_att[:, 2, :], ACT.Copy, scale=-1.0).then_inc(s("gdn_nw"), 1)
                act.wait_ge(s("gdn_nw"), made("gdn_nw"))
                fill(2)
                for c in range(NT):
                    fill(1)
                act.wait_ge(s("gdn_o"), h + 1)
                act.activation(sq[:, 0, :], v_tmp[:], ACT.Square).then_inc(s("gdn_osq"), 1)
                act.wait_ge(s("gdn_osq"), made("gdn_osq"))

            def gdn_rms(h):
                act.wait_ge(s("gdn_oss"), h + 1)
                if h:
                    act.wait_ge(s("gdn_on"), h)
                root(sq[:, 2, :], ps_aux[:], "gdn_rno")

            pieces = iter(())
            for r in range(GDN_H + 1):
                done = 0

                def fill(n):
                    nonlocal done, pieces
                    if r < GDN_H:
                        for k in range(done, min(done + n, 4 * ND)):
                            if k % ND == ND - 1:
                                for _ in pieces:
                                    pass
                                pieces = gdn_tile(r, k // ND)
                    done += n
                    next(pieces, None)
                if r:
                    gdn_head(r - 1, fill)
                while done < 4 * ND:
                    fill(1)
                for _ in pieces:
                    pass
            gdn_rms(GDN_H - 1)
            norm([tile_of("gdn_w_out", m) for m in range(ND)])

            F = swa
            act.dma_start(F["q"].bitcast(i32), a["positions"]).then_inc(s("pos_in"), 16)
            act.wait_ge(s("swa_angle"), 1)
            step(act.activation(F["cos"], F["sin"], ACT.Abs))
            act.activation(F["cos"], F["cos"], ACT.Sin, scale=-1.0, bias=float(np.pi / 2)).then_inc(s("swa_sin"), 1)
            act.wait_ge(s("swa_sin"), made("swa_sin"))
            act.activation(F["sin"], F["sin"], ACT.Sin).then_inc(s("swa_sin"), 1)
            act.wait_ge(s("swa_sin"), made("swa_sin"))
            for j in range(ND):
                act.wait_ge(bank_read(tile_of("swa_w_in", 12 + j)), reads(tile_of("swa_w_in", 12 + j)))
                act.activation(F["z"][:, j % 2, :], F["z"][:, j % 2, :], ACT.Silu).then_inc(s("z_silu"), 1)
                act.wait_ge(s("z_silu"), made("z_silu"))
                for half in range(2):
                    n, L, st = 2 * j + half, F["L"][half], F["st"][:, 4 * half:4 * half + 4, :]
                    act.wait_ge(s("swa_max"), n + 1)
                    act.activation(L[:, 0, P:], L[:, 0, P:], ACT.Exp, bias=st[:, 0, 0:1], accum_out=st[:, 1, 0:1])
                    for i in range(1, NT):
                        act.activation(L[:, i, :], L[:, i, :], ACT.Exp, bias=st[:, 0, i:i + 1], accum_out=st[:, 1, i:i + 1])
                    act.activation(st[:, 2, :], st[:, 0, :], ACT.Exp, bias=sinks[:, n:n + 1]).then_inc(s("swa_exp"), 1)
                if j:
                    act.wait_ge(s("swa_o"), j)
                for half in range(2):
                    for pairs in range(2):
                        act.wait_ge(s("swa_ptT"), 2 * (2 * j + half) + pairs + 1)
                        b0, nb = (0, 3) if pairs == 0 else (3, 4)
                        act.activation(F["PT"][:, half, b0:b0 + nb, :].rearrange("p b c -> p (b c)"), ps_att[:, 2 * half + pairs, 0:nb * P], ACT.Copy).then_inc(s("swa_pt"), 1)
            act.wait_ge(s("swa_pt"), 4 * ND)
            norm([tile_of("swa_w_out", m) for m in range(ND)])
            norm()

            F = ml
            R4 = slice(0, 4)
            act.wait_ge(s("softplus_in"), 3)
            step(act.activation(F["em"][R4, :], F["r1"][R4, :], ACT.Abs))
            step(act.activation(F["em"][R4, :], F["em"][R4, :], ACT.Exp, scale=-1.0))
            act.activation(F["em"][R4, :], F["em"][R4, :], ACT.Ln, bias=1.0).then_inc(s("softplus_out"), 1)
            act.wait_ge(s("softplus_out"), made("softplus_out"))
            act.wait_ge(bank_read(tile_of("w_mem_kv_2", XA_H - 1)), reads(tile_of("w_mem_kv_2", XA_H - 1)))
            act.activation(sq[:, 0:2, :].rearrange("p a b -> p (a b)"), mem_k.rearrange("p a b -> p (a b)"), ACT.Square).then_inc(s("xa_ksq"), 1)
            for g in range(2):
                act.wait_ge(s("xa_kss"), g + 1)
                root(F["ST"][:, g * T:(g + 1) * T], ps_att[:, g, :], "xa_krn")
            for r in range(ML_H + 1):
                h = r - 1
                for part in range(4):
                    if h >= 0:
                        if part == 0:
                            act.wait_ge(s("ml_bc"), h + 1)
                            act.activation(F["M"], ps_aux[:], ACT.Copy).then_inc(s("ml_M"), 1)
                            act.wait_ge(s("ml_M"), made("ml_M"))
                            act.wait_ge(s("ml_bcm"), h + 1)
                            act.activation(F["em"], ps_att[:, 3, :], ACT.Exp).then_inc(s("ml_em"), 1)
                            act.wait_ge(s("ml_em"), made("ml_em"))
                            for j in range(NT):
                                act.wait_ge(s("ml_diff"), NT * h + j + 1)
                                d = F["ST"][:, OFF[j]:OFF[j] + T - j * P]
                                act.activation(d, d, ACT.Exp).then_inc(s("ml_decay"), 1)
                                act.wait_ge(s("ml_decay"), made("ml_decay"))
                        if part == 1:
                            act.wait_ge(s("ml_vT"), h + 1)
                            act.activation(F["vt"].rearrange("p a b -> p (a b)"), ps_aux[:], ACT.Copy).then_inc(s("ml_v"), 1)
                            act.wait_ge(s("ml_v"), made("ml_v"))
                        if part == 2:
                            act.wait_ge(s("ml_pv"), h + 1)
                            act.activation(F["den"], ps_att[:, 1, :], ACT.Abs).then_inc(s("ml_abs"), 1)
                            act.wait_ge(s("ml_abs"), made("ml_abs"))
                            act.wait_ge(s("ml_h"), h + 1)
                            act.activation(sq[:, 0, :], F["t2"], ACT.Square).then_inc(s("ml_sq"), 1)
                            act.wait_ge(s("ml_sq"), made("ml_sq"))
                        if part == 3:
                            act.wait_ge(s("ml_ss"), h + 1)
                            root(F["rn"], ps_aux[:], "ml_rn")
                    if r < ML_H:
                        t = tile_of("w_ml", part * ML_H + r)
                        if part < 2:
                            act.wait_ge(s("ml_conv"), 2 * r + part + 1)
                            act.activation((F["q"] if part == 0 else F["k"])[:, r % 2, :], F["t"], ACT.Silu).then_inc(s("ml_silu"), 1)
                            act.wait_ge(s("ml_silu"), made("ml_silu"))
                        elif part == 3:
                            act.wait_ge(bank_read(t), reads(t))
                            act.activation(F["o"][:, r % 2, :], F["o"][:, r % 2, :], ACT.Tanh, scale=0.5).then_inc(s("ml_tanh"), 1)
                            act.wait_ge(s("ml_tanh"), made("ml_tanh"))

            F = sbk
            def sb_logs(n):
                L, t = F["L"][n % 2], F["W"][n % 4]
                for b in range(NT):
                    act.wait_ge(s("sb_z"), NT * n + b + 1)
                    act.activation(L[:, OFF[b]:OFF[b] + T - b * P], ps_att[:, b, b * P:], ACT.Copy, scale=HD ** -0.5).then_inc(s("sb_L"), 1)
                act.wait_ge(s("sb_L"), NT * (n + 1))
                if n > 3:
                    act.wait_ge(s("sb_o"), (n - 4) // 2 + 1)
                step(act.activation(t, L, ACT.Abs))
                step(act.activation(t, t, ACT.Exp, scale=-1.0))
                act.activation(t, t, ACT.Ln, bias=1.0).then_inc(s("sb_log"), 1)

            sb_logs(0)
            for n in range(SB_H):
                if n < SB_H - 1:
                    sb_logs(n + 1)
                act.wait_ge(s("sb_logw"), NT * (n + 1))
                act.activation(F["W"][n % 4], F["L"][n % 2], ACT.Exp).then_inc(s("sb_exp"), 1)
                act.wait_ge(s("sb_exp"), n + 1)

            F = xa

            def xa_square(h):
                act.wait_ge(bank_read(tile_of("w_xa", h)), reads(tile_of("w_xa", h)))
                act.activation(sq[:, h % 3, :], F["q"][:, h, :], ACT.Square).then_inc(s("xa_qsq"), 1)

            def xa_root(h):
                act.wait_ge(s("xa_qss"), h + 1)
                if h:
                    act.wait_ge(s("xa_q"), h)
                root(F["n"], ps_aux[:], "xa_qrn")

            def gate(n):
                act.wait_ge(bank_read(tile_of("w_gate", n)), reads(tile_of("w_gate", n)))
                act.activation(mg["sg"][:, n % 2, :], mg["sg"][:, n % 2, :], ACT.Tanh, scale=0.5).then_inc(s("gate_tanh"), 1)

            act.wait_ge(s("sb_o"), SB_H // 2)
            for h in range(XA_H - 1):
                xa_square(h)
            xa_root(0)
            xa_square(XA_H - 1)
            for h in range(XA_H):
                st = F["st"]
                if h < XA_H - 1:
                    xa_root(h + 1)
                act.wait_ge(s("xa_max"), h + 1)
                for i in range(NT):
                    last = act.activation(F["L"][:, i, :], ps_att[:, i // 2, (i % 2) * MEM:(i % 2 + 1) * MEM], ACT.Exp, scale=XA_HD ** -0.5, bias=st[:, 0, i:i + 1], accum_out=st[:, 1, i:i + 1])
                last.then_inc(s("xa_exp"), 1)
                gate(2 * h)
                gate(2 * h + 1)
            for n in range(2 * XA_H, 3 * ND):
                gate(n)
            norm([tile_of("w_o_2", m) for m in range(ND)])

            for c in range(NF):
                act.wait_ge(s("ff_gate"), c + 1)
                act.activation(ff["s"][:, c % 2, :], ff["tg"][:, c % 2, :], ACT.Silu).then_inc(s("ff_silu"), 1)
                act.wait_ge(s("ff_silu"), made("ff_silu"))

        @block.tensor
        def _(pe):
            waited = {}

            def need(name, n):
                if n > waited.get(name, 0):
                    pe.wait_ge(s(name), n)
                    waited[name] = n

            at = [0, 0]
            y_layer = {"conv_w_out": 0, "fox_w_out": 1, "gdn_w_out": 2, "swa_w_out": 3}

            def project(chunks):
                for _ in range(chunks):
                    n, k = at
                    weight, i, k0, kc, c, operand, tokens, first, last, t = UNITS[n]
                    slot, bank, kk = n % SPLIT, t % BANKS, k0 + k
                    if k == 0:
                        need("w_split", 2 * (n + 1))
                        if first and t >= BANKS:
                            need(f"evacuated{bank}", reads(t - BANKS))
                    if operand.startswith("xw"):
                        need("xw_ready", ND * int(operand[2:]) + kk + 1)
                        hi, lo = xw_hi[:, kk, :], xw_lo[:, kk, :]
                    elif operand == "mem":
                        need("mem_ready", kk + 1)
                        hi, lo = (z[:, 8 + kk // 2, (kk % 2) * MEM:(kk % 2 + 1) * MEM] for z in (y_hi, y_lo))
                    else:
                        base = {"w_ml_out_2": 4, "w_xa_out_2": 8}.get(operand, 0)
                        ready = {"w_sb_out_2": ("sb_y", kk + 1), "w_ml_out_2": ("ml_y", kk + 1), "w_xa_out_2": ("xa_y", kk + 1),
                                 "merged": ("merged", kk + 1), "u": ("u_ready", kk + 1)}.get(operand)
                        need(*(ready or ("y_ready", ND * y_layer[weight] + kk + 1)))
                        hi, lo = y_hi[:, (base + kk) % 12, :], y_lo[:, (base + kk) % 12, :]
                    wh, wl = w_hi[:, slot, k * c:(k + 1) * c], w_lo[:, slot, k * c:(k + 1) * c]
                    o = ps_lin[0:c, bank, 0:tokens]
                    pe.matmul(o, wh, hi, start=first and k == 0, stop=False)
                    pe.matmul(o, wh, lo, start=False, stop=False)
                    ins = pe.matmul(o, wl, hi, start=False, stop=last and k == kc - 1)
                    if k == kc - 1:
                        ins.then_inc(s("unit_done"), 1)
                    at[:] = (n, k + 1) if k < kc - 1 else (n + 1, 0)

            def tile(n=1):
                for _ in range(n):
                    t = UNITS[at[0]][9]
                    while at[0] < len(UNITS) and UNITS[at[0]][9] == t:
                        project(1)

            aux_reader = [("mats_in", 16)]

            def aux(reader, n):
                last, aux_reader[0] = aux_reader[0], (reader, n)
                return s(last[0]), last[1]

            def mm(o, l, r, start=True, stop=True):
                return pe.matmul(o, l, r, start=start, stop=stop)

            def tr(o, i, n=P):
                return pe.transpose(o, i, mat("ident")[0:n, 0:n])

            def spread(o, rws, n, h):
                return mm(o, mat("ident")[0:n, h:h + 1].to_broadcast([n, P]), rws[0:n, :])

            def sum_squares(k):
                pe.wait_ge(*aux("rstd_ready", k + 1))
                pe.wait_ge(s("sq_added"), (ND - 1) * (k + 1))
                mm(ps_aux[:], mat("mean_d"), sq[:, 0, :]).then_inc(s("ss_done"), 1)

            pe.wait_ge(s("mats_in"), 16)
            tile(2)
            sum_squares(0)
            pe.wait_ge(*aux("rstd_mem", 1))
            pe.wait_ge(s("mem_added"), ND - 1)
            mm(ps_aux[:, 0:MEM], mat("mean_d"), sq[:, 0, 0:MEM]).then_inc(s("mem_ss"), 1)

            tile(4 * ND - 2)
            tile(ND)
            tile(2)
            sum_squares(1)

            F = fox
            for r in range(FOX_H + 1):
                h = r - 1
                b = h % 2
                if 0 < r < FOX_H:
                    tile()
                if h >= 0:
                    pe.wait_ge(s("fox_c"), 1)
                    pe.wait_ge(*aux("fox_cb", h + 1))
                    spread(ps_aux[:], F["c"], 8, h).then_inc(s("fox_bc"), 1)
                    pe.wait_ge(bank_read(tile_of("fox_w_in", h)), reads(tile_of("fox_w_in", h)))
                    pe.wait_ge(bank_read(tile_of("fox_w_in", 8 + h)), reads(tile_of("fox_w_in", 8 + h)))
                    pe.wait_ge(s("fox_pt_dve"), 2 * h)
                    pe.wait_ge(s("fox_pt_act"), 2 * h)
                    for i in range(NT):
                        mm(ps_att[:, i, 0:(i + 1) * P], blk(F["q"][:, b, :], i), F["k"][:, b, 0:(i + 1) * P]).then_inc(s("fox_scores"), 1)
                if r < FOX_H:
                    tile()
                if h >= 0:
                    pe.wait_ge(bank_read(tile_of("fox_w_in", 16 + h)), reads(tile_of("fox_w_in", 16 + h)))
                    pe.wait_ge(*aux("fox_v", h + 1))
                    for i in range(NT):
                        last = tr(blk(ps_aux, i), blk(F["v"][:, b, :], i))
                        if i == NT - 1:
                            last.then_inc(s("fox_vT"), 1)
                if r < FOX_H:
                    tile()
                if h >= 0:
                    pe.wait_ge(s("fox_scored"), NT * (h + 1))
                    for j in range(NT):
                        for i in range(j, NT):
                            pe.wait_ge(s("fox_p"), NT * h + i + 1)
                            last = tr(blk(ps_att[:, j, :], i), blk(F["L"][:, i, :], j))
                            if i == NT - 1:
                                last.then_inc(s("fox_pt"), 1)
                if r < FOX_H:
                    tile()
                if h >= 0:
                    pe.wait_ge(*aux("head_out", h + 1))
                    for j in range(NT):
                        pe.wait_ge(s("fox_pt_act" if j % 2 else "fox_pt_dve"), 2 * h + j // 2 + 1)
                        last = mm(ps_aux[:, j * P:], F["vt"][:, j, :], F["PT"][:, j, j * P:], j == 0, j == NT - 1)
                        if j == NT - 1:
                            last.then_inc(s("fox_o"), 1)
            tile(ND)
            tile(2)
            sum_squares(2)

            F = gdn
            EARLY = 2 * ND - 1
            project(EARLY)
            pe.wait_ge(s("rows_ready"), 1)
            pe.wait_ge(*aux("columns", 1))
            for i, name in enumerate(("beta", "be", "el", "r2")):
                for c in range(NT):
                    last = tr(ps_aux[:, (i * NT + c) * 8:(i * NT + c + 1) * 8], blk(F[name][0:8, :], c), n=8)
                    if i == 3 and c == NT - 1:
                        last.then_inc(s("rows_turned"), 1)

            def gdn_tile(r, part):
                if part in (1, 2):
                    pe.wait_ge(s("gdn_sq"), 2 * r + part)
                    pe.wait_ge(*aux("gdn_rn", 2 * r + part))
                    mm(ps_aux[:], mat("ones"), sq[:, 1, :]).then_inc(s("gdn_ss"), 1)

            def four(o, l, r, start=True, stop=True):
                for c in range(NT):
                    last = mm(blk(o, c), l(c), r(c), start, stop)
                return last

            def gdn_head(h, fill):
                q_, k_, v_, z_ = (F[n][:, h % 2, :] for n in "qkvz")
                X, Y, Z, V = (ps_att[:, i, :] for i in range(4))
                B = lambda name: (lambda c: blk(F[name], c))
                pe.wait_ge(s("gdn_nw"), h)
                pe.wait_ge(s("gdn_vb"), h)
                spread(Z, F["g"], 8, h).then_inc(s("gdn_bc"), 1)
                spread(V, F["beta"], 8, h).then_inc(s("gdn_bc"), 1)
                fill(1)
                if h:
                    gdn_squares(h - 1)
                fill(1)
                pe.wait_ge(s("gdn_kb"), h + 1)
                pe.wait_ge(s("gdn_bcG"), h + 1)
                pe.wait_ge(s("gdn_o"), h)
                pe.wait_ge(s("gdn_vn_out"), NT * h)
                four(X, lambda c: blk(k_, c), B("kb")).then_inc(s("gdn_A"), 1)
                four(Y, lambda c: blk(k_, c), lambda c: blk(q_, c)).then_inc(s("gdn_A"), 1)
                fill(2)
                for l in range(7):
                    if l:
                        for g in range(2):
                            pe.wait_ge(s("gdn_T"), 12 * h + 2 * l - 1 + g)
                            for c in (2 * g, 2 * g + 1):
                                last = mm(blk(ps_att[:, 2 * g, :], c % 2), blk(F["LT"], c), blk(F["Tm"], c))
                            last.then_inc(s("gdn_XT"), 1)
                        fill(1)
                        if l == 1:
                            pe.wait_ge(s("gdn_QK"), h + 1)
                        for g in range(2):
                            pe.wait_ge(s("gdn_X"), 12 * h + 2 * l - 1 + g)
                            for c in (2 * g, 2 * g + 1):
                                last = mm(blk(ps_att[:, 2 * g + 1, :], c % 2), blk(F["X"], c), blk(F["U"], c))
                            last.then_inc(s("gdn_XU"), 1)
                        fill(1)
                    if l < 6:
                        for g in range(2):
                            pe.wait_ge(s("gdn_U"), 14 * h + 2 * l + 1 + g)
                            for c in (2 * g, 2 * g + 1):
                                last = tr(blk(ps_att[:, 2 * g, :], c % 2), blk(F["U"], c))
                            last.then_inc(s("gdn_UT"), 1)
                    fill(1)
                fill(1)
                for c in range(NT):
                    tr(blk(X, c), blk(k_, c))
                pe.wait_ge(s("gdn_U"), 14 * h + 14)
                for c in range(NT):
                    last = tr(blk(V, c), blk(v_, c))
                    if c == NT - 1:
                        last.then_inc(s("gdn_tok"), 1)
                pe.wait_ge(s("gdn_kbg"), h + 1)
                pe.wait_ge(s("gdn_U"), 14 * h + 14)
                four(Z, B("kbg"), B("U")).then_inc(s("gdn_w"), 1)
                fill(2)
                pe.wait_ge(s("gdn_vb"), h + 1)
                for c in range(NT):
                    last = mm(blk(Y, c), blk(F["U"], c), blk(F["vb"], c), True, not c)
                    if not (c):
                        last.then_inc(s("gdn_vn"), 1)
                    if c:
                        pe.wait_ge(s("gdn_nw"), h + 1)
                        pe.wait_ge(s("gdn_state"), (NT - 1) * h + c)
                        mm(blk(Y, c), blk(F["nwT"], c), F["S"], False, True).then_inc(s("gdn_vn"), 1)
                        mm(blk(X, c), F["S"], blk(F["qd"], c), True, False)
                    pe.wait_ge(s("gdn_vn_out"), NT * h + c + 1)
                    if c < NT - 1:
                        pe.wait_ge(*aux("gdn_state", (NT - 1) * h + c + 1))
                        mm(ps_aux[:, 0:P], blk(F["kd"], c), blk(F["vn"], c)).then_inc(s("gdn_S"), 1)
                    last = mm(blk(X, c), blk(F["vn"], c), blk(F["QK"], c), not c, True)
                    if c == NT - 1:
                        last.then_inc(s("gdn_out"), 1)
                    fill(1)

            def gdn_squares(h):
                pe.wait_ge(*aux("gdn_rno", h + 1))
                pe.wait_ge(s("gdn_osq"), h + 1)
                mm(ps_aux[:], mat("mean_h"), sq[:, 0, :]).then_inc(s("gdn_oss"), 1)

            for r in range(GDN_H + 1):
                done = [0 if r else EARLY]

                def fill(n, r=r, done=done):
                    if r < GDN_H:
                        for k in range(done[0], min(done[0] + n, 4 * ND)):
                            project(1)
                            if k % ND == ND - 1:
                                gdn_tile(r, k // ND)
                    done[0] += n
                if r:
                    gdn_head(r - 1, fill)
                fill(max(0, 4 * ND - done[0]))
            gdn_squares(GDN_H - 1)
            tile(ND)
            tile(2)
            sum_squares(3)

            F = swa
            for kt in range(2):
                t = tile_of("swa_w_in", 8 + kt)
                pe.wait_ge(bank_read(t), reads(t))
                pe.wait_ge(s("gdn_o"), GDN_H)
                pe.wait_ge(s("gdn_nw"), GDN_H)
                pe.wait_ge(s("swa_k"), 2 * kt)
                for g in range(2):
                    mm(ps_att[:, 2 * g, :], mat(f"dup{g}"), F["q"])
                    mm(ps_att[:, 2 * g + 1, :], mat(f"duprot{g}"), F["q"]).then_inc(s("swa_kdup"), 1)
                tile()
            for vt in range(2):
                pe.wait_ge(bank_read(tile_of("swa_w_in", 10 + vt)), reads(tile_of("swa_w_in", 10 + vt)))
                pe.wait_ge(*aux("swa_v", 4 * (vt + 1)))
                for i in range(NT):
                    last = tr(blk(ps_aux, i), blk(F["q"], i))
                    if i == NT - 1:
                        last.then_inc(s("swa_vT"), 1)
                tile()
            def swa_rotate(j):
                pe.wait_ge(bank_read(tile_of("swa_w_in", j)), reads(tile_of("swa_w_in", j)))
                pe.wait_ge(*aux("swa_q", j + 1))
                mm(ps_aux[:], mat("rot"), F["qr"]).then_inc(s("swa_qrot"), 1)

            def swa_pv(j):
                pe.wait_ge(*aux("head_out", j + 9))
                pe.wait_ge(s("swa_pt"), 4 * (j + 1))
                for i in range(NT):
                    steps = [(half, b) for half in range(2) for b in ((i - 1, i) if i else (0,))]
                    for k, (half, b) in enumerate(steps):
                        piece = 0 if i == 0 else 2 * i - 1 + (b == i)
                        last = mm(blk(ps_aux, i), blk(F["vp"][:, j // 2, half, :], b), F["PT"][:, half, piece, :], k == 0, k == len(steps) - 1)
                        if i == NT - 1 and k == len(steps) - 1:
                            last.then_inc(s("swa_o"), 1)

            swa_rotate(0)
            for j in range(ND):
                pe.wait_ge(s("swa_q"), j + 1)
                for half in range(2):
                    d = slice(half * HD, (half + 1) * HD)
                    kj = F["k"][d, j // 2, :]
                    if j:
                        pe.wait_ge(s("swa_pt"), 2 * (2 * (j - 1) + half + 1))
                    else:
                        pe.wait_ge(s("swa_k"), 4)
                    for i in range(NT):
                        lo = max(0, i - 1)
                        last = mm(ps_att[:, 2 * half + i // 2, SWA_BASE[i]:SWA_BASE[i] + (i + 1 - lo) * P], blk(F["q"][d, :], i), kj[:, lo * P:(i + 1) * P])
                        if i % 2:
                            last.then_inc(s("swa_scores"), 1)
                if j:
                    swa_pv(j - 1)
                if j < ND - 1:
                    tile()
                for half in range(2):
                    pe.wait_ge(s("swa_p"), 2 * j + half + 1)
                    for i in range(NT):
                        ps, base = ps_att[:, 2 * half + i // 2, :], SWA_BASE[i]
                        for part in range(0 if i else 1, 2):
                            last = tr(ps[:, base:base + P], F["L"][half][:, i, part * P:(part + 1) * P])
                            if i % 2 and part:
                                last.then_inc(s("swa_ptT"), 1)
                            base += P
                    if j < ND - 1 and half == 0:
                        swa_rotate(j + 1)
                        tile()
            swa_pv(ND - 1)
            tile(ND)

            tile(2)
            sum_squares(4)
            tile(ND - 2)
            sum_squares(5)
            tile(2)

            F = ml
            EARLY = 3
            tile(EARLY)
            pe.wait_ge(s("rows_ready"), 2)
            pe.wait_ge(*aux("columns", 2))
            for j in range(NT):
                last = tr(ps_aux[:, j * 4:(j + 1) * 4], blk(F["g"][0:4, :], j), n=4)
                if j == NT - 1:
                    last.then_inc(s("rows_turned"), 1)
            pe.wait_ge(s("xa_ksq"), 1)
            for g in range(2):
                mm(ps_att[:, g, :], mat("mean_h"), sq[:, g, :]).then_inc(s("xa_kss"), 1)
            pe.wait_ge(bank_read(tile_of("w_mem_kv_2", 2 * XA_H - 1)), reads(tile_of("w_mem_kv_2", 2 * XA_H - 1)))
            pe.wait_ge(bank_read(tile_of("w_mem_kv_2", 2 * XA_H - 2)), reads(tile_of("w_mem_kv_2", 2 * XA_H - 2)))
            for i in range(2 * XA_H):
                last = tr(blk(ps_att[:, 2 + i // 4, :], i % 4), blk(mem_v[:, i // 2, :], i % 2))
                if i % 4 == 3:
                    last.then_inc(s("xa_vT"), 1)
            for r in range(ML_H + 1):
                h = r - 1
                b = h % 2
                for part in range(4):
                    if h >= 0:
                        if part == 0:
                            pe.wait_ge(*aux("ml_M", h + 1))
                            spread(ps_aux[:], F["nm"], 4, h).then_inc(s("ml_bc"), 1)
                            pe.wait_ge(s("xa_v"), 2)
                            pe.wait_ge(s("xa_k"), 2)
                            pe.wait_ge(s("ml_st"), NT * h)
                            spread(ps_att[:, 3, :], F["m"], 4, h).then_inc(s("ml_bcm"), 1)
                            pe.wait_ge(s("ml_silu"), 2 * h + 2)
                            pe.wait_ge(s("ml_h"), h)
                            for j in range(NT):
                                if j == 3:
                                    pe.wait_ge(s("ml_em"), h + 1)
                                mm(ps_att[:, j, j * P:], blk(F["k"][:, b, :], j), F["q"][:, b, j * P:]).then_inc(s("ml_scores"), 1)
                        if part == 1:
                            pe.wait_ge(bank_read(tile_of("w_ml", 2 * ML_H + h)), reads(tile_of("w_ml", 2 * ML_H + h)))
                            pe.wait_ge(*aux("ml_v", h + 1))
                            for j in range(NT):
                                last = tr(blk(ps_aux, j), blk(F["v"], j))
                                if j == NT - 1:
                                    last.then_inc(s("ml_vT"), 1)
                        if part == 2:
                            pe.wait_ge(s("ml_v"), h + 1)
                            pe.wait_ge(s("ml_st"), NT * (h + 1))
                            for j in range(NT):
                                mm(ps_att[:, 0, j * P:], F["vt"][:, j, :], F["ST"][:, OFF[j]:OFF[j] + T - j * P], j == 0, j == NT - 1)
                            for j in range(NT):
                                last = mm(ps_att[:, 1, j * P:], mat("ones"), F["ST"][:, OFF[j]:OFF[j] + T - j * P], j == 0, j == NT - 1)
                                if j == NT - 1:
                                    last.then_inc(s("ml_pv"), 1)
                        if part == 3:
                            pe.wait_ge(*aux("ml_rn", h + 1))
                            pe.wait_ge(s("ml_sq"), h + 1)
                            mm(ps_aux[:], mat("mean_h"), sq[:, 0, :]).then_inc(s("ml_ss"), 1)
                    if 0 < r < ML_H or r == 0 and part >= EARLY:
                        tile()

            F = sbk

            def sb_scores(n):
                j, d = n // 2, slice(n % 2 * HD, (n % 2 + 1) * HD)
                pe.wait_ge(bank_read(tile_of("w_sb", j)), reads(tile_of("w_sb", j)))
                pe.wait_ge(bank_read(tile_of("w_sb", 4 + j)), reads(tile_of("w_sb", 4 + j)))
                if n:
                    pe.wait_ge(s("sb_L"), NT * n)
                    pe.wait_ge(s("sb_logw"), NT * (n - 1))
                for b in range(NT):
                    mm(ps_att[:, b, b * P:], blk(F["k"][d, j % 2, :], b), F["q"][d, j % 2, b * P:]).then_inc(s("sb_z"), 1)

            def sb_sums(n):
                pe.wait_ge(s("sb_sp"), NT * (n + 1))
                pe.wait_ge(s("sb_L"), NT * min(n + 2, SB_H))
                sp = F["W"][n % 4]
                for b in range(NT):
                    last = mm(ps_att[:, b, b * P:], mat("neg_lower_incl"), sp[:, OFF[b]:OFF[b] + T - b * P], True, b == NT - 1)
                    for k in range(b + 1, NT):
                        last = mm(ps_att[:, b, k * P:], mat("neg_ones"), sp[:, OFF[k]:OFF[k] + T - k * P], False, k == NT - 1)
                    last.then_inc(s("sb_after"), 1)

            def sb_pv(j):
                pe.wait_ge(s("sb_W"), 2 * NT * (j + 1))
                pe.wait_ge(*aux("head_out", j + 17))
                for half in range(2):
                    for b in range(NT):
                        end = half == 1 and b == NT - 1
                        last = mm(ps_aux[:, b * P:], F["vp"][:, half, b, :], F["W"][(2 * j + half) % 4][:, OFF[b]:OFF[b] + T - b * P], half == 0 and b == 0, end)
                        if end:
                            last.then_inc(s("sb_o"), 1)

            tile(3)
            pe.wait_ge(s("ml_h"), ML_H)
            sb_scores(0)
            for n in range(SB_H):
                j, even = n // 2, n % 2 == 0
                more = j < SB_H // 2 - 1
                if n < SB_H - 1:
                    sb_scores(n + 1)
                tile()
                if even:
                    if j:
                        sb_pv(j - 1)
                    pe.wait_ge(bank_read(tile_of("w_sb", 8 + j)), reads(tile_of("w_sb", 8 + j)))
                    pe.wait_ge(*aux("sb_v", 2 * (j + 1)))
                    for i in range(NT):
                        last = tr(blk(ps_aux, i), blk(F["v"], i))
                    last.then_inc(s("sb_vT"), 1)
                sb_sums(n)
                if more and even:
                    tile()
            tile()
            sb_pv(SB_H // 2 - 1)

            F = xa

            def xa_squares(h):
                pe.wait_ge(*aux("xa_qrn", h + 1))
                pe.wait_ge(s("xa_qsq"), h + 1)
                mm(ps_aux[:], mat("mean_h"), sq[:, h % 3, :]).then_inc(s("xa_qss"), 1)

            xa_squares(0)
            tile()
            for h in range(XA_H):
                pe.wait_ge(s("xa_q"), h + 1)
                for i in range(NT):
                    last = mm(ps_att[:, i // 2, (i % 2) * MEM:(i % 2 + 1) * MEM], blk(F["q"][:, h, :], i), mem_k[:, h, :])
                    if i % 2:
                        last.then_inc(s("xa_scores"), 1)
                if h < XA_H - 1:
                    xa_squares(h + 1)
                tile(2)
                pe.wait_ge(s("xa_p"), h + 1)
                pe.wait_ge(s("xa_pt"), 2 * h)
                for b in range(2):
                    for i in range(NT):
                        last = tr(blk(ps_att[:, 2 + b, :], i), F["L"][:, i, b * P:(b + 1) * P])
                    last.then_inc(s("xa_ptT"), 1)
                tile(2)
                pe.wait_ge(s("xa_pt"), 2 * (h + 1))
                pe.wait_ge(*aux("head_out", h + 21))
                for b in range(2):
                    last = mm(ps_aux[:], blk(mem_v[:, h, :], b), F["PT"][:, b, :], not b, bool(b))
                last.then_inc(s("xa_o"), 1)

            tile(4 * ND)
            tile(ND)
            tile(2)
            sum_squares(6)
            while at[0] < len(UNITS):
                project(1)


def column(v):
    return np.ascontiguousarray(v.reshape(-1, P).T)


def weight_tiles(w, cols=P):
    k, n = w.shape
    return np.ascontiguousarray(w.reshape(k // P, P, n // cols, cols).transpose(2, 1, 0, 3).reshape(n // cols, P, -1))


def kernel(**inputs):
    from concourse import bacc
    from concourse.bass_utils import run_bass_kernel_spmd

    i = {k: np.asarray(v) for k, v in inputs.items()}
    fox, gdn, win = i["fox_w_in"][0], i["gdn_w_in"][0], i["w_in_2"][0]
    at = np.cumsum([0, 512, 512, 512, 512, 512, 512, 512, 4, 4, 512, 3072])
    arrays = {
        "x": np.ascontiguousarray(i["x"][0].T.reshape(ND, P, T)),
        "mem": np.ascontiguousarray(i["mem_2"][0].T.reshape(ND, P, MEM).transpose(1, 0, 2).reshape(P, -1)),
        "positions": np.ascontiguousarray(np.broadcast_to(i["positions"], (P, T))),
        "sinks": np.ascontiguousarray(np.broadcast_to(i["swa_sinks"], (P, SWA_H))),
        "freq": inv_freq(), "mats": constants(),
        "cols": np.ascontiguousarray(np.concatenate([column(i[n]) for n, _ in COL_NAMES], axis=1)),
        "rows": np.ascontiguousarray(np.stack([np.resize(i[n][0], 8) for n in ROW_NAMES], axis=1)),
        "fox_w_f": weight_tiles(fox[:, 4096:], FOX_H), "fox_w_in": weight_tiles(fox[:, :4096]),
        "gdn_w_beta": weight_tiles(gdn[:, 4096:4104], 8), "gdn_w_a": weight_tiles(gdn[:, 4104:], 8),
        "gdn_w_in": weight_tiles(gdn[:, :4096]),
        "w_sb": weight_tiles(win[:, 0:at[3]]), "w_ml": weight_tiles(win[:, at[3]:at[7]]),
        "ml_w_i": weight_tiles(win[:, at[7]:at[8]], 4), "ml_w_f": weight_tiles(win[:, at[8]:at[9]], 4),
        "w_xa": weight_tiles(win[:, at[9]:at[10]]), "w_gate": weight_tiles(win[:, at[10]:]),
    }
    for n in WEIGHTS:
        if n not in arrays:
            arrays[n] = weight_tiles(i[n][0])
    nc = bacc.Bacc("TRN2", target_bir_lowering=False, num_devices=1)
    args = {n: nc.dram_tensor("in_" + n, v.shape, mybir.dt.from_np(v.dtype), kind="ExternalInput").ap() for n, v in arrays.items()}
    out = nc.dram_tensor("out", (ND, P, T), mybir.dt.float32, kind="ExternalOutput").ap()
    block_program(nc, args, out)
    r = run_bass_kernel_spmd(nc, [{"in_" + n: v for n, v in arrays.items()}], core_ids=[0])
    return np.ascontiguousarray(r.results[0]["out"].reshape(D, T).T)[None]
```
